# Optimizing a Trainium2 kernel written in Bass

```python
import math
import jax, jax.numpy as jnp
from jax import lax
import numpy as np

D_MODEL = 1024
BATCH = 1
SEQ = 1024
DEPTH = 1

PLE_DIM = 256
BRANCH_WIDTH = D_MODEL // 2
HEAD_DIM = 128
RET_HEADS = BRANCH_WIDTH // HEAD_DIM
GDN_HEADS = BRANCH_WIDTH // HEAD_DIM
LRU_WIDTH = BRANCH_WIDTH
LRU_BLOCKS = 8
LRU_C = 8.0
CONV_WIDTH = 4
CHUNK = 64
N_BRANCHES = 3
ROPE_BASE = 10000.0
N_EXPERTS = 64
TOP_K = 8
N_GROUPS = 8
TOPK_GROUPS = 4
EXPERT_FF = 256
SHARED_FF = 256
ROUTED_SCALE = 2.5
MOE_BLOCK = 256
LN_EPS = 1e-5
DN_ALPHA = (2 * DEPTH) ** 0.25
DN_BETA = (8 * DEPTH) ** -0.25
IN_SPLITS = (BRANCH_WIDTH, BRANCH_WIDTH, BRANCH_WIDTH, BRANCH_WIDTH,
             3 * BRANCH_WIDTH, BRANCH_WIDTH, GDN_HEADS, GDN_HEADS,
             LRU_WIDTH, LRU_WIDTH,
             N_BRANCHES * D_MODEL)
D_IN = sum(IN_SPLITS)

kernel_name = 'hybrid_ret_gdn_rglru_moe_deepnorm'

def layer_norm(x, g, b):
    xf = x.astype(jnp.float32)
    mu = xf.mean(-1, keepdims=True)
    var = jnp.square(xf - mu).mean(-1, keepdims=True)
    return ((xf - mu) * lax.rsqrt(var + LN_EPS) * g + b).astype(x.dtype)

def causal_dwconv(x, w):
    c = x.shape[-1]
    return lax.conv_general_dilated(x, w[:, None, :].astype(x.dtype), window_strides=(1,),
                                    padding=[(w.shape[0] - 1, 0)],
                                    dimension_numbers=('NWC', 'WIO', 'NWC'), feature_group_count=c)

def to_chunks(t):
    b, s, h, d = t.shape
    return t.reshape(b, s // CHUNK, CHUNK, h, d).transpose(0, 3, 1, 2, 4)

def from_chunks(t):
    b, h, n, c, d = t.shape
    return t.transpose(0, 2, 3, 1, 4).reshape(b, n * c, h, d)

def rotary(x):
    s, d = x.shape[1], x.shape[-1]
    inv_freq = ROPE_BASE ** (-jnp.linspace(0.0, 1.0, d // 2, dtype=jnp.float32))
    ang = jnp.arange(s, dtype=jnp.float32)[:, None] * inv_freq[None, :]
    cos = jnp.cos(ang)[None, :, None, :]
    sin = jnp.sin(ang)[None, :, None, :]
    x1, x2 = x[..., : d // 2], x[..., d // 2:]
    return jnp.concatenate([x1 * cos - x2 * sin, x2 * cos + x1 * sin], axis=-1)

def l2norm(x):
    return x * lax.rsqrt(jnp.sum(x * x, axis=-1, keepdims=True) + 1e-6)

def retention(q, k, v):
    b, s, h, dk = q.shape
    log_gamma = jnp.log1p(-jnp.exp2(-5.0 - jnp.arange(h, dtype=jnp.float32)))
    q = rotary(q)
    k = rotary(k) * (dk ** -0.5)
    qc, kc, vc = to_chunks(q), to_chunks(k), to_chunks(v)
    pos = jnp.arange(CHUNK, dtype=jnp.float32)
    diff = pos[:, None] - pos[None, :]
    causal = diff >= 0
    intra_decay = jnp.where(causal, jnp.exp(log_gamma[:, None, None] * jnp.where(causal, diff, 0.0)), 0.0)
    scores = jnp.einsum('bhncd,bhnmd->bhncm', qc, kc) * intra_decay[None, :, None]
    o_intra = jnp.einsum('bhncm,bhnmv->bhncv', scores, vc)
    q_decay = jnp.exp(log_gamma[:, None] * (pos + 1.0))[None, :, :, None]
    k_decay = jnp.exp(log_gamma[:, None] * (CHUNK - 1.0 - pos))[None, :, :, None]
    chunk_decay = jnp.exp(log_gamma * CHUNK)[None, :, None, None]

    def step(state, xs):
        q_n, k_n, v_n = xs
        o_n = jnp.einsum('bhcd,bhdv->bhcv', q_n * q_decay, state)
        state = state * chunk_decay + jnp.einsum('bhcd,bhcv->bhdv', k_n * k_decay, v_n)
        return state, o_n

    state0 = jnp.zeros((b, h, dk, v.shape[-1]), jnp.float32)
    _, o_inter = lax.scan(step, state0, (jnp.moveaxis(qc, 2, 0), jnp.moveaxis(kc, 2, 0), jnp.moveaxis(vc, 2, 0)))
    return from_chunks(o_intra + jnp.moveaxis(o_inter, 0, 2))

def gated_delta_rule(q, k, v, beta, log_alpha):
    b, s, h, dk = q.shape
    q = q * (dk ** -0.5)
    qc, kc, vc = to_chunks(q), to_chunks(k), to_chunks(v)
    bc = to_chunks(beta[..., None])[..., 0]
    gc = jnp.cumsum(to_chunks(log_alpha[..., None])[..., 0], axis=-1)
    lower = jnp.tril(jnp.ones((CHUNK, CHUNK), bool))
    strict = jnp.tril(jnp.ones((CHUNK, CHUNK), bool), -1)
    gdiff = gc[..., :, None] - gc[..., None, :]
    decay = jnp.where(lower, jnp.exp(jnp.where(lower, gdiff, 0.0)), 0.0)
    kb = kc * bc[..., None]
    a_strict = jnp.where(strict, jnp.einsum('bhncd,bhnmd->bhncm', kb, kc) * decay, 0.0)
    t_mat = a_strict + jnp.eye(CHUNK, dtype=jnp.float32)
    u = lax.linalg.triangular_solve(t_mat, vc * bc[..., None], left_side=True, lower=True, unit_diagonal=True)
    w = lax.linalg.triangular_solve(t_mat, kb * jnp.exp(gc)[..., None], left_side=True, lower=True, unit_diagonal=True)
    qk = jnp.einsum('bhncd,bhnmd->bhncm', qc, kc) * decay
    q_dec = qc * jnp.exp(gc)[..., None]
    k_dec = kc * jnp.exp(gc[..., -1:] - gc)[..., None]
    g_last = jnp.exp(gc[..., -1])[..., None, None]

    def step(state, xs):
        u_n, w_n, qk_n, qd_n, kd_n, gl_n = xs
        v_new = u_n - jnp.einsum('bhcd,bhdv->bhcv', w_n, state)
        o_n = jnp.einsum('bhcd,bhdv->bhcv', qd_n, state) + jnp.einsum('bhcm,bhmv->bhcv', qk_n, v_new)
        state = state * gl_n + jnp.einsum('bhcd,bhcv->bhdv', kd_n, v_new)
        return state, o_n

    xs = (jnp.moveaxis(u, 2, 0), jnp.moveaxis(w, 2, 0), jnp.moveaxis(qk, 2, 0),
          jnp.moveaxis(q_dec, 2, 0), jnp.moveaxis(k_dec, 2, 0), jnp.moveaxis(g_last, 2, 0))
    state0 = jnp.zeros((b, h, dk, v.shape[-1]), jnp.float32)
    _, o = lax.scan(step, state0, xs)
    return from_chunks(jnp.moveaxis(o, 0, 2))

def rg_lru(x, w_r, b_r, w_i, b_i, lam):
    b, s, wdt = x.shape
    xb = x.reshape(b, s, LRU_BLOCKS, wdt // LRU_BLOCKS)
    r = jax.nn.sigmoid(jnp.einsum('bsgi,gij->bsgj', xb, w_r.astype(jnp.float32)).reshape(b, s, wdt) + b_r)
    i = jax.nn.sigmoid(jnp.einsum('bsgi,gij->bsgj', xb, w_i.astype(jnp.float32)).reshape(b, s, wdt) + b_i)
    log_a = -LRU_C * r * jax.nn.softplus(-lam.astype(jnp.float32))
    a = jnp.exp(log_a)
    gated_in = jnp.sqrt(-jnp.expm1(2.0 * log_a)) * (i * x)

    def combine(left, right):
        a1, h1 = left
        a2, h2 = right
        return a1 * a2, a2 * h1 + h2

    _, h = lax.associative_scan(combine, (a, gated_in), axis=1)
    return h

def hybrid_mixer(h, w_in, b_in, ret_norm_g, ret_norm_b, gdn_conv_w, gdn_a_log, gdn_dt_bias, gdn_norm_g,
                 lru_conv_w, lru_conv_b, lru_w_r, lru_b_r, lru_w_i, lru_b_i, lru_lambda, w_branch, w_out):
    b, s, d = h.shape
    f32 = jnp.float32
    split_at = [int(c) for c in np.cumsum(IN_SPLITS)[:-1]]
    (rq, rk, rv, rg, gqkv, gg, gb, ga, lx, lg, mg) = jnp.split(h @ w_in + b_in, split_at, axis=-1)

    o_ret = retention(rq.astype(f32).reshape(b, s, RET_HEADS, HEAD_DIM),
                      rk.astype(f32).reshape(b, s, RET_HEADS, HEAD_DIM),
                      rv.astype(f32).reshape(b, s, RET_HEADS, HEAD_DIM))
    mu = o_ret.mean(-1, keepdims=True)
    var = jnp.square(o_ret - mu).mean(-1, keepdims=True)
    o_ret = ((o_ret - mu) * lax.rsqrt(var + LN_EPS)).reshape(b, s, BRANCH_WIDTH) * ret_norm_g + ret_norm_b
    y_ret = jax.nn.silu(rg.astype(f32)) * o_ret

    qkv = jax.nn.silu(causal_dwconv(gqkv, gdn_conv_w)).astype(f32)
    gq, gk, gv = jnp.split(qkv, 3, axis=-1)
    q = l2norm(gq.reshape(b, s, GDN_HEADS, HEAD_DIM))
    k = l2norm(gk.reshape(b, s, GDN_HEADS, HEAD_DIM))
    v = gv.reshape(b, s, GDN_HEADS, HEAD_DIM)
    beta = jax.nn.sigmoid(gb.astype(f32))
    log_alpha = -jnp.exp(gdn_a_log.astype(f32)) * jax.nn.softplus(ga.astype(f32) + gdn_dt_bias)
    o_gdn = gated_delta_rule(q, k, v, beta, log_alpha)
    o_gdn = o_gdn * lax.rsqrt(jnp.mean(o_gdn * o_gdn, axis=-1, keepdims=True) + 1e-6) * gdn_norm_g
    y_gdn = (o_gdn * jax.nn.silu(gg.astype(f32).reshape(b, s, GDN_HEADS, HEAD_DIM))).reshape(b, s, BRANCH_WIDTH)

    xc = (causal_dwconv(lx, lru_conv_w) + lru_conv_b).astype(f32)
    y_lru = jax.nn.gelu(lg.astype(f32)) * rg_lru(xc, lru_w_r, lru_b_r, lru_w_i, lru_b_i, lru_lambda)

    branches = jnp.stack([y_ret, y_gdn, y_lru], axis=2).astype(h.dtype)
    branches = jnp.einsum('bsnw,nwd->bsnd', branches, w_branch)
    gates = jax.nn.sigmoid(mg.reshape(b, s, N_BRANCHES, d))
    return jnp.sum(gates * branches, axis=2) @ w_out

def swiglu(x, w_gu, w_down):
    gate, up = jnp.split(x @ w_gu, 2, axis=-1)
    return (jax.nn.silu(gate) * up) @ w_down

def routed_experts(xt, eidx, gw, w_gu, w_down):
    n, d = xt.shape
    e = w_gu.shape[0]
    k = eidx.shape[1]
    a = n * k
    flat_e = eidx.reshape(-1)
    flat_t = jnp.repeat(jnp.arange(n, dtype=jnp.int32), k)
    flat_w = gw.reshape(-1).astype(xt.dtype)
    order = jnp.argsort(flat_e)
    se = flat_e[order]
    counts = jnp.zeros((e,), jnp.int32).at[flat_e].add(1)
    starts = jnp.cumsum(counts) - counts
    padded = (counts + MOE_BLOCK - 1) // MOE_BLOCK * MOE_BLOCK
    pends = jnp.cumsum(padded)
    pstarts = pends - padded
    dest = pstarts[se] + jnp.arange(a, dtype=jnp.int32) - starts[se]
    n_blocks = -(-a // MOE_BLOCK) + e
    rows = n_blocks * MOE_BLOCK
    row_tok = jnp.full((rows,), n, jnp.int32).at[dest].set(flat_t[order])
    row_w = jnp.zeros((rows,), xt.dtype).at[dest].set(flat_w[order])
    blk_start = jnp.arange(n_blocks, dtype=jnp.int32) * MOE_BLOCK
    blk_e = jnp.minimum(jnp.searchsorted(pends, blk_start, side='right'), e - 1).astype(jnp.int32)
    x_pad = jnp.concatenate([xt, jnp.zeros((1, d), xt.dtype)], axis=0)

    def block(acc, inp):
        tok, wt, ex = inp
        y = swiglu(x_pad[tok], w_gu[ex], w_down[ex])
        return acc.at[tok].add((y * wt[:, None]).astype(acc.dtype)), None

    out, _ = lax.scan(block, jnp.zeros((n + 1, d), xt.dtype),
                      (row_tok.reshape(n_blocks, MOE_BLOCK), row_w.reshape(n_blocks, MOE_BLOCK), blk_e))
    return out[:n]

def moe(x, router_w, router_b, exp_w_gu, exp_w_down, sh_w_gu, sh_w_down):
    b, s, d = x.shape
    xt = x.reshape(b * s, d)
    n = xt.shape[0]
    scores = jax.nn.sigmoid((xt @ router_w).astype(jnp.float32))
    sel = scores + router_b.astype(jnp.float32)
    grp_score = lax.top_k(sel.reshape(n, N_GROUPS, N_EXPERTS // N_GROUPS), 2)[0].sum(-1)
    _, gidx = lax.top_k(grp_score, TOPK_GROUPS)
    gmask = jax.nn.one_hot(gidx, N_GROUPS, dtype=jnp.float32).sum(1) > 0
    emask = jnp.repeat(gmask, N_EXPERTS // N_GROUPS, axis=1)
    _, eidx = lax.top_k(jnp.where(emask, sel, -jnp.inf), TOP_K)
    gw = jnp.take_along_axis(scores, eidx, axis=1)
    gw = gw / jnp.sum(gw, axis=-1, keepdims=True) * ROUTED_SCALE
    routed = routed_experts(xt, eidx, gw, exp_w_gu, exp_w_down)
    shared = swiglu(xt, sh_w_gu, sh_w_down)
    return (routed + shared).reshape(b, s, d)

def setup_inputs(seed: int = 0) -> dict:
    key = jax.random.key(seed)
    ks = iter(jax.random.split(key, 40))
    L, D, W, H = DEPTH, D_MODEL, BRANCH_WIDTH, GDN_HEADS
    nrm = lambda shape, scale: jax.random.normal(next(ks), shape, jnp.float32) * scale
    gain = lambda shape: 1.0 + nrm(shape, 0.02)
    dt = jnp.exp(jax.random.uniform(next(ks), (L, H), jnp.float32, math.log(0.001), math.log(0.1)))
    a0 = jax.random.uniform(next(ks), (L, LRU_WIDTH), jnp.float32, 0.9, 0.999)
    a_base = a0 ** (1.0 / LRU_C)
    return {
        'x': nrm((BATCH, SEQ, D), 1.0),
        'p': nrm((DEPTH, BATCH, SEQ, PLE_DIM), 1.0),
        'ln_in_g': gain((D,)),
        'ln_in_b': nrm((D,), 0.02),
        'w_in': nrm((L, D, D_IN), D ** -0.5),
        'b_in': nrm((L, D_IN), 0.02),
        'ret_norm_g': gain((L, W)),
        'ret_norm_b': nrm((L, W), 0.02),
        'gdn_conv_w': nrm((L, CONV_WIDTH, 3 * W), CONV_WIDTH ** -0.5),
        'gdn_a_log': jnp.log(jax.random.uniform(next(ks), (L, H), jnp.float32, 1.0, 16.0)),
        'gdn_dt_bias': dt + jnp.log(-jnp.expm1(-dt)),
        'gdn_norm_g': gain((L, HEAD_DIM)),
        'lru_conv_w': nrm((L, CONV_WIDTH, LRU_WIDTH), CONV_WIDTH ** -0.5),
        'lru_conv_b': nrm((L, LRU_WIDTH), 0.02),
        'lru_w_r': nrm((L, LRU_BLOCKS, LRU_WIDTH // LRU_BLOCKS, LRU_WIDTH // LRU_BLOCKS), (LRU_WIDTH // LRU_BLOCKS) ** -0.5),
        'lru_b_r': nrm((L, LRU_WIDTH), 0.02),
        'lru_w_i': nrm((L, LRU_BLOCKS, LRU_WIDTH // LRU_BLOCKS, LRU_WIDTH // LRU_BLOCKS), (LRU_WIDTH // LRU_BLOCKS) ** -0.5),
        'lru_b_i': nrm((L, LRU_WIDTH), 0.02),
        'lru_lambda': jnp.log(a_base) - jnp.log1p(-a_base),
        'w_branch': nrm((L, N_BRANCHES, W, D), W ** -0.5),
        'w_out': nrm((L, D, D), D ** -0.5 * DN_BETA),
        'ln1_g': gain((L, D)),
        'ln1_b': nrm((L, D), 0.02),
        'router_w': nrm((L, D, N_EXPERTS), D ** -0.5),
        'router_b': nrm((L, N_EXPERTS), 0.01),
        'exp_w_gu': nrm((L, N_EXPERTS, D, 2 * EXPERT_FF), D ** -0.5),
        'exp_w_down': nrm((L, N_EXPERTS, EXPERT_FF, D), EXPERT_FF ** -0.5 * DN_BETA),
        'sh_w_gu': nrm((L, D, 2 * SHARED_FF), D ** -0.5),
        'sh_w_down': nrm((L, SHARED_FF, D), SHARED_FF ** -0.5 * DN_BETA),
        'ple_w_e': nrm((L, PLE_DIM, D), PLE_DIM ** -0.5 * DN_BETA),
        'ple_w_g': nrm((L, D, D), D ** -0.5),
        'ple_b_g': nrm((L, D), 0.02),
        'ln2_g': gain((L, D)),
        'ln2_b': nrm((L, D), 0.02),
    }

def reference(x, p, ln_in_g, ln_in_b, w_in, b_in, ret_norm_g, ret_norm_b, gdn_conv_w, gdn_a_log, gdn_dt_bias,
              gdn_norm_g, lru_conv_w, lru_conv_b, lru_w_r, lru_b_r, lru_w_i, lru_b_i, lru_lambda, w_branch, w_out,
              ln1_g, ln1_b, router_w, router_b, exp_w_gu, exp_w_down, sh_w_gu, sh_w_down, ple_w_e, ple_w_g,
              ple_b_g, ln2_g, ln2_b):
    h = layer_norm(x, ln_in_g, ln_in_b)
    for l in range(DEPTH):
        mix = hybrid_mixer(h, w_in[l], b_in[l], ret_norm_g[l], ret_norm_b[l], gdn_conv_w[l], gdn_a_log[l],
                           gdn_dt_bias[l], gdn_norm_g[l], lru_conv_w[l], lru_conv_b[l], lru_w_r[l], lru_b_r[l],
                           lru_w_i[l], lru_b_i[l], lru_lambda[l], w_branch[l], w_out[l])
        h = layer_norm(DN_ALPHA * h + mix, ln1_g[l], ln1_b[l])
        ffn = moe(h, router_w[l], router_b[l], exp_w_gu[l], exp_w_down[l], sh_w_gu[l], sh_w_down[l])
        ple = jax.nn.sigmoid(h @ ple_w_g[l] + ple_b_g[l]) * (p[l].astype(h.dtype) @ ple_w_e[l])
        h = layer_norm(DN_ALPHA * h + ffn + ple, ln2_g[l], ln2_b[l])
    return h


_drawn_inputs = setup_inputs


def setup_inputs(seed=0):
    import zlib

    import numpy as np

    out = dict(_drawn_inputs(seed))
    spreads = {}
    factors = {'ret_norm_g': 3.495,
     'ret_norm_b': 3.008,
     'gdn_norm_g': 3.996,
     'lru_b_r': 28.074,
     'lru_b_i': 27.242,
     'ple_b_g': 30.666,
     'ln2_g': 7.539,
     'ln2_b': 7.802}
    for name, (base, spread) in spreads.items():
        noise = np.random.default_rng([zlib.crc32(name.encode()), seed]).standard_normal(out[name].shape)
        drawn = base * np.exp(spread * noise) if base else spread * noise
        out[name] = __import__('jax').numpy.asarray(drawn.astype(out[name].dtype))
    for name, factor in factors.items():
        out[name] = (out[name] * factor).astype(out[name].dtype)
    return out
```

```python
import math
from contextlib import ExitStack

import numpy as np

import concourse.bass as bass
from concourse import mybir

F32 = mybir.dt.float32
ALU = mybir.AluOpType
ACT = mybir.ActivationFunctionType
AX = mybir.AxisListType

P = 128
SEQ = 1024
D = 1024
NT = SEQ // P
KD = D // P
W = 512
H = 4
CH = W // P
HALF = 512
NE = 64
FF = 256
TOPK = 8
NG = 8
GS = NE // NG
PLE = 256
LEVELS = 7
LN_EPS = 1e-5
ALPHA = 2.0 ** 0.25
LRU_C = 8.0
ROUTED_SCALE = 2.5

C_RQ, C_RK, C_RV, C_RG = 0, W, 2 * W, 3 * W
C_QKV = 4 * W
C_GG = C_QKV + 3 * W
C_BA = C_GG + W
C_LX = C_BA + 2 * H
C_LG = C_LX + W
C_MG = C_LG + W

COLS = {}


def _col_plan():
    at = 0
    for name, n in (("b_rg", 4), ("b_qkv", 12), ("b_gg", 4), ("b_lx", 4), ("b_lg", 4), ("b_mg", 24),
                    ("ret_g", 4), ("ret_b", 4), ("gdn_w", 48), ("gdn_g", 1), ("lru_w", 16), ("lru_cb", 4),
                    ("lru_br", 4), ("lru_bi", 4), ("lru_lam", 4)):
        COLS[name] = (at, n)
        at += n
    return at


N_COLS = _col_plan()

CONSTS = {}


def _const_plan():
    at = 0
    for name, n in (("ident", P), ("upper", P), ("level", LEVELS * P), ("rmask", H * P), ("rqdec", H * P),
                    ("rkdec", H), ("cos", NT * 64), ("sin", NT * 64)):
        CONSTS[name] = (at, n)
        at += n
    return at


N_CONSTS = _const_plan()
GAMMA = [1.0 - 2.0 ** (-5 - h) for h in range(H)]


def constant_table():
    out = np.zeros((P, N_CONSTS), np.float32)

    def put(name, a):
        at, n = CONSTS[name]
        out[:, at:at + n] = np.asarray(a, np.float32).reshape(P, n)

    i = np.arange(P)
    row, col = i[:, None], i[None, :]
    put("ident", np.eye(P))
    put("upper", row <= col)
    level = np.zeros((P, LEVELS, P))
    for s in range(LEVELS):
        b = 1 << s
        level[:, s, :] = (row // (2 * b) == col // (2 * b)) & ((col // b) % 2 == 1) & ((row // b) % 2 == 0)
    put("level", level)
    scale = float(P) ** -0.5
    lg = np.log1p(-np.exp2(-5.0 - np.arange(H)))
    diff = col - row
    rmask = np.zeros((P, H, P))
    qdec = np.zeros((P, H, P))
    for h in range(H):
        rmask[:, h, :] = np.where(diff >= 0, np.exp(lg[h] * np.maximum(diff, 0)), 0.0) * scale
        qdec[:, h, :] = np.exp(lg[h] * (col + 1.0))
    put("rmask", rmask)
    put("rqdec", qdec)
    put("rkdec", np.exp(lg[None, :] * (P - 1.0 - row)) * scale)
    inv = np.float32(10000.0) ** (-np.linspace(0.0, 1.0, 64, dtype=np.float32))
    ang = np.arange(SEQ, dtype=np.float32)[:, None] * inv[None, :].astype(np.float32)
    put("cos", np.cos(ang.astype(np.float32)).reshape(NT, P, 64).transpose(1, 0, 2))
    put("sin", np.sin(ang.astype(np.float32)).reshape(NT, P, 64).transpose(1, 0, 2))
    return out


def chained(eng, sem, start=0):
    n = [start]

    def link(ins):
        n[0] += 1
        ins.then_inc(sem, 1)
        eng.wait_ge(sem, n[0])
    return link


def build(nc, a, out, dbg=None):
    ctx = ExitStack()
    with ctx:
        stage_sems = []

        def sem(name):
            stage_sems.append(nc.alloc_semaphore(name=name))
            return stage_sems[-1]

        def end_stage():
            nc.all_engine_barrier()
            nc.clear_and_free_semaphores(list(stage_sems))
            stage_sems.clear()
            nc.all_engine_barrier()

        A = ctx.enter_context(nc.sbuf_tensor("arena", [P, 53000], F32))
        PS = ctx.enter_context(nc.psum_tensor("banks", [P, 8, 512], F32))
        h_d = nc.dram_tensor("h_scratch", (P, NT, D), F32).ap()
        y_d = {n: nc.dram_tensor(f"y_{n}_scratch", (P, CH, SEQ), F32).ap() for n in ("ret", "gdn", "lru")}

        top = [0]

        def carve(n, at=None):
            at0 = top[0] if at is None else at
            if at is None:
                top[0] += n
            assert at0 + n <= 53000, (at0, n)
            return A[:, at0:at0 + n]

        cst = carve(N_CONSTS)
        cols = carve(N_COLS)

        def const(name):
            at, n = CONSTS[name]
            return cst[:, at:at + n]

        def col(name, i, n=1):
            at, _ = COLS[name]
            return cols[:, at + i:at + i + n]

        ident = const("ident")
        nhalf = carve(64)
        upper = const("upper")
        hT = carve(KD * SEQ).rearrange("p (k s) -> p k s", k=KD)
        base = top[0]

        def region():
            top[0] = base

        def tok3(ap):
            return ap.rearrange("p (t c) -> p t c", t=NT)

        def row(name, lo, n):
            return a[name][lo:lo + n].rearrange("(a n) -> a n", a=1).broadcast_to([P, n])

        w_in = a["w_in"]

        def w_cols(lo, n):
            return w_in[:, lo:lo + n].rearrange("(k p) n -> p k n", p=P)

        def ln_stats(v, link, src, st, mv, t):
            for j in range(2):
                link(nc.vector.bn_stats(st[:, t, j, :], src[:, t, j * HALF:(j + 1) * HALF]))
            return nc.vector.bn_aggr(mv[:, t, :], st[:, t, :, :])

        def ln_apply(link, dst, t, mv, rstd, g_row, b_row):
            link(nc.vector.tensor_scalar(dst[:, t, :], dst[:, t, :], mv[:, t, 0:1], rstd[:, t:t + 1],
                                         ALU.subtract, ALU.mult))
            link(nc.vector.tensor_tensor(dst[:, t, :], dst[:, t, :], g_row, ALU.mult))
            return nc.vector.tensor_tensor(dst[:, t, :], dst[:, t, :], b_row, ALU.add)

        def transpose_tiles(pe, src, ready, moved, freed):
            for t in range(NT):
                pe.wait_ge(ready, t + 1)
                for j in range(2):
                    i = 2 * t + j
                    if i >= 4:
                        pe.wait_ge(freed, i - 3)
                    for c in range(4):
                        k = 4 * j + c
                        last = nc.tensor.transpose(PS[:, i % 4, c * P:(c + 1) * P], src[:, t, k * P:(k + 1) * P], ident)
                    last.then_inc(moved, 1)

        def copy_transposed(act, dst, moved, freed):
            for i in range(2 * NT):
                t, j = i // 2, i % 2
                act.wait_ge(moved, i + 1)
                nc.scalar.activation(dst[:, 4 * j:4 * j + 4, t * P:(t + 1) * P],
                                     PS[:, i % 4, :].rearrange("p (c s) -> p c s", c=4), ACT.Copy).then_inc(freed, 1)

        region()
        h = tok3(carve(NT * D))
        g_row, b_row = carve(D), carve(D)
        st = carve(NT * 12).rearrange("p (t j s) -> p t j s", t=NT, j=2)
        mv = carve(NT * 2).rearrange("p (t s) -> p t s", t=NT)
        rstd = carve(NT)
        a_par, a_x, a_chain = sem("a_params"), [sem(f"a_x{i}") for i in range(4)], sem("a_chain")
        a_stat, a_rstd, a_h, a_tp, a_hT, a_st = (sem(n) for n in ("a_stat", "a_rstd", "a_h", "a_tp", "a_hT", "a_store"))
        with nc.Block() as block:
            @block.sync
            def _(sp):
                xv = a["x"][0].rearrange("(t p) d -> p t d", p=P)
                for i in range(4):
                    sp.dma_start(h[:, 2 * i:2 * i + 2, :], xv[:, 2 * i:2 * i + 2, :]).then_inc(a_x[i], 16)
                sp.wait_ge(a_h, NT)
                sp.dma_start(h_d, h).then_inc(a_st, 16)
                sp.wait_ge(a_st, 16)

            @block.scalar
            def _(act):
                act.dma_start(cst, a["consts"]).then_inc(a_par, 16)
                act.dma_start(cols, a["cols"]).then_inc(a_par, 16)
                act.dma_start(g_row, row("ln_in_g", 0, D)).then_inc(a_par, 16)
                act.dma_start(b_row, row("ln_in_b", 0, D)).then_inc(a_par, 16)
                copy_transposed(act, hT, a_tp, a_hT)

            @block.vector
            def _(v):
                link = chained(v, a_chain)
                for t in range(NT):
                    v.wait_ge(a_x[t // 2], 16)
                    ln_stats(v, link, h, st, mv, t).then_inc(a_stat, 1)
                v.wait_ge(a_rstd, 3)
                v.wait_ge(a_par, 64)
                for t in range(NT):
                    ln_apply(link, h, t, mv, rstd, g_row, b_row).then_inc(a_h, 1)

            @block.gpsimd
            def _(pool):
                nc.gpsimd.memset(nhalf, -0.5).then_inc(a_rstd, 1)
                pool.wait_ge(a_stat, NT)
                nc.gpsimd.tensor_scalar(rstd, mv[:, :, 1], LN_EPS, None, ALU.add).then_inc(a_rstd, 1)
                pool.wait_ge(a_rstd, 2)
                nc.gpsimd.tensor_tensor(rstd, rstd, nhalf[:, 0:NT], ALU.pow).then_inc(a_rstd, 1)

            @block.tensor
            def _(pe):
                pe.wait_ge(a_par, 64)
                transpose_tiles(pe, h, a_h, a_tp, a_hT)

        region()
        q3, k3, v3 = (tok3(carve(NT * W)) for _ in range(3))
        yr = carve(CH * SEQ).rearrange("p (c s) -> p c s", c=CH)
        ring = [carve(KD * W).rearrange("p (k n) -> p k n", k=KD) for _ in range(2)]
        bias3 = carve(3 * W)
        qr, kr, kd, ta, tb = (carve(W) for _ in range(5))
        qTs, kTs, qTd, sT, cen, sq, on, yt = (carve(W) for _ in range(8))
        S = [carve(W) for _ in range(2)]
        stat4 = carve(3 * H)
        r_w = [sem("r_w0"), sem("r_w1")]
        (r_par, r_grp, r_job, r_evD, r_evA, r_chain, r_rot, r_tq, r_tk, r_qT, r_kT, r_qTd, r_sc, r_sT, r_dS, r_S,
         r_o, r_var, r_rstd, r_on, r_to, r_yt, r_y, r_st) = (sem("r_" + n) for n in (
             "par", "grp", "job", "evD", "evA", "chain", "rot", "tq", "tk", "qT", "kT", "qTd", "sc", "sT", "dS", "S",
             "o", "var", "rstd", "on", "to", "yt", "y", "st"))
        R_GROUPS = (C_RQ, C_RK, C_RV, C_RG)

        def heads(ap):
            return ap.rearrange("p (h c) -> p h c", h=H)

        def per_head(ap4, n=P):
            return ap4.unsqueeze(2).broadcast_to([P, H, n])

        def project_tokens(pe, wt, bank, t):
            for k in range(KD):
                last = nc.tensor.matmul(PS[:, bank, :], hT[:, k, t * P:(t + 1) * P], wt[:, k, :],
                                        start=(k == 0), stop=(k == KD - 1))
            return last

        def project_channels(pe, wt, bank, ct, half):
            for k in range(KD):
                last = nc.tensor.matmul(PS[:, bank, :], wt[:, k, ct * P:(ct + 1) * P],
                                        hT[:, k, half * HALF:(half + 1) * HALF],
                                        start=(k == 0), stop=(k == KD - 1))
            return last

        with nc.Block() as block:
            @block.sync
            def _(sp):
                for g, c0 in enumerate(R_GROUPS):
                    if g >= 2:
                        sp.wait_ge(r_grp, g - 1)
                    sp.dma_start(ring[g % 2], w_cols(c0, W)).then_inc(r_w[g % 2], 16)
                    if g == 0:
                        sp.dma_start(bias3, row("b_in", 0, 3 * W)).then_inc(r_par, 16)
                sp.wait_ge(r_y, NT)
                sp.dma_start(y_d["ret"], yr).then_inc(r_st, 16)
                sp.wait_ge(r_st, 16)

            @block.tensor
            def _(pe):
                def freed(job):
                    if job < 0:
                        return
                    if job < 24:
                        pe.wait_ge(r_evD, job + 1)
                    else:
                        pe.wait_ge(r_evA, job - 23)

                for g in range(4):
                    pe.wait_ge(r_w[g % 2], 16 * (g // 2 + 1))
                    for j in range(8):
                        job = 8 * g + j
                        freed(job - 2)
                        if g < 3:
                            last = project_tokens(pe, ring[g % 2], job % 2, j)
                        else:
                            last = project_channels(pe, ring[g % 2], job % 2, j // 2, j % 2)
                        last.then_inc(r_job, 1)
                    pe.wait_ge(r_job, 8 * (g + 1))
                    pe.sem_inc(r_grp, 1)
                for t in range(NT):
                    pe.wait_ge(r_rot, t + 1)
                    if t:
                        pe.wait_ge(r_qT, t)
                        pe.wait_ge(r_kT, t)
                    for hh in range(H):
                        last = nc.tensor.transpose(PS[:, 2, hh * P:(hh + 1) * P], qr[:, hh * P:(hh + 1) * P], ident)
                    last.then_inc(r_tq, 1)
                    for hh in range(H):
                        last = nc.tensor.transpose(PS[:, 3, hh * P:(hh + 1) * P], kr[:, hh * P:(hh + 1) * P], ident)
                    last.then_inc(r_tk, 1)
                    if t:
                        pe.wait_ge(r_S, t)
                    for hh in range(H):
                        hs = slice(hh * P, (hh + 1) * P)
                        last = nc.tensor.matmul(PS[:, 6, hs], kd[:, hs], v3[:, t, hs], start=True, stop=True)
                    last.then_inc(r_dS, 1)
                    pe.wait_ge(r_qT, t + 1)
                    pe.wait_ge(r_kT, t + 1)
                    if t:
                        pe.wait_ge(r_sT, t)
                    for hh in range(H):
                        hs = slice(hh * P, (hh + 1) * P)
                        last = nc.tensor.matmul(PS[:, 4, hs], kTs[:, hs], qTs[:, hs], start=True, stop=True)
                    last.then_inc(r_sc, 1)
                    pe.wait_ge(r_sT, t + 1)
                    if t:
                        pe.wait_ge(r_qTd, t + 1)
                        pe.wait_ge(r_S, t)
                        pe.wait_ge(r_on, t)
                    for hh in range(H):
                        hs = slice(hh * P, (hh + 1) * P)
                        last = nc.tensor.matmul(PS[:, 5, hs], sT[:, hs], v3[:, t, hs], start=True, stop=(t == 0))
                        if t:
                            last = nc.tensor.matmul(PS[:, 5, hs], qTd[:, hs], S[t % 2][:, hs], start=False, stop=True)
                    last.then_inc(r_o, 1)
                    pe.wait_ge(r_on, t + 1)
                    if t:
                        pe.wait_ge(r_yt, t)
                    for hh in range(H):
                        hs = slice(hh * P, (hh + 1) * P)
                        last = nc.tensor.transpose(PS[:, 7, hs], on[:, hs], ident)
                    last.then_inc(r_to, 1)

            @block.scalar
            def _(act):
                for j in range(8):
                    act.wait_ge(r_job, 24 + j + 1)
                    nc.scalar.activation(yr[:, j // 2, (j % 2) * HALF:(j % 2 + 1) * HALF], PS[:, j % 2, :], ACT.Silu,
                                         bias=col("b_rg", j // 2)).then_inc(r_evA, 1)
                for t in range(NT):
                    act.wait_ge(r_tq, t + 1)
                    if t:
                        act.wait_ge(r_sc, t)
                        act.wait_ge(r_qTd, t)
                    nc.scalar.activation(qTs, PS[:, 2, :], ACT.Copy).then_inc(r_qT, 1)
                    act.wait_ge(r_tk, t + 1)
                    nc.scalar.activation(kTs, PS[:, 3, :], ACT.Copy).then_inc(r_kT, 1)
                    act.wait_ge(r_to, t + 1)
                    if t:
                        act.wait_ge(r_y, t)
                    for hh in range(H):
                        hs = slice(hh * P, (hh + 1) * P)
                        last = nc.scalar.activation(yt[:, hs], PS[:, 7, hs], ACT.Identity,
                                                    bias=col("ret_b", hh), scale=col("ret_g", hh))
                    last.then_inc(r_yt, 1)

            @block.vector
            def _(v):
                link = chained(v, r_chain)
                v.wait_ge(r_par, 16)
                for job in range(24):
                    g, t = job // 8, job % 8
                    v.wait_ge(r_job, job + 1)
                    nc.vector.tensor_tensor((q3, k3, v3)[g][:, t, :], PS[:, job % 2, :],
                                            bias3[:, g * W:(g + 1) * W], ALU.add).then_inc(r_evD, 1)
                v.wait_ge(r_evD, 24)
                for t in range(NT):
                    cos_t = const("cos")[:, t * 64:(t + 1) * 64]
                    sin_t = const("sin")[:, t * 64:(t + 1) * 64]
                    if t:
                        v.wait_ge(r_tk, t)
                        v.wait_ge(r_dS, t)
                    for src, dst in ((q3, qr), (k3, kr)):
                        x4 = src[:, t, :].rearrange("p (h f c) -> p h f c", h=H, f=2)
                        d4 = dst.rearrange("p (h f c) -> p h f c", h=H, f=2)
                        a4 = ta.rearrange("p (h f c) -> p h f c", h=H, f=2)
                        b4 = tb.rearrange("p (h f c) -> p h f c", h=H, f=2)
                        cb = cos_t.unsqueeze(1).broadcast_to([P, H, 64])
                        sb_ = sin_t.unsqueeze(1).broadcast_to([P, H, 64])
                        nc.vector.tensor_tensor(a4[:, :, 0, :], x4[:, :, 0, :], cb, ALU.mult)
                        nc.vector.tensor_tensor(a4[:, :, 1, :], x4[:, :, 1, :], cb, ALU.mult)
                        nc.vector.tensor_tensor(b4[:, :, 0, :], x4[:, :, 1, :], sb_, ALU.mult)
                        link(nc.vector.tensor_tensor(b4[:, :, 1, :], x4[:, :, 0, :], sb_, ALU.mult))
                        nc.vector.tensor_tensor(d4[:, :, 0, :], a4[:, :, 0, :], b4[:, :, 0, :], ALU.subtract)
                        link(nc.vector.tensor_tensor(d4[:, :, 1, :], a4[:, :, 1, :], b4[:, :, 1, :], ALU.add))
                    nc.vector.tensor_tensor(heads(kd), heads(kr), per_head(const("rkdec")), ALU.mult).then_inc(r_rot, 1)
                    v.wait_ge(r_qT, t + 1)
                    if t:
                        v.wait_ge(r_o, t)
                    nc.vector.tensor_tensor(qTd, qTs, const("rqdec"), ALU.mult).then_inc(r_qTd, 1)
                    v.wait_ge(r_sc, t + 1)
                    nc.vector.tensor_tensor(sT, PS[:, 4, :], const("rmask"), ALU.mult).then_inc(r_sT, 1)
                    v.wait_ge(r_dS, t + 1)
                    for hh in range(H):
                        hs = slice(hh * P, (hh + 1) * P)
                        if t == 0:
                            last = nc.vector.tensor_copy(S[1][:, hs], PS[:, 6, hs])
                        else:
                            last = nc.vector.scalar_tensor_tensor(S[(t + 1) % 2][:, hs], S[t % 2][:, hs],
                                                                  GAMMA[hh] ** P, PS[:, 6, hs], ALU.mult, ALU.add)
                    link(last)
                    last = nc.vector.memset(stat4[:, 0:1], 0.0)
                    last.then_inc(r_S, 1)
                    v.wait_ge(r_S, t + 1)
                    v.wait_ge(r_o, t + 1)
                    mean, var, rs = stat4[:, 0:H], stat4[:, H:2 * H], stat4[:, 2 * H:3 * H]
                    link(nc.vector.tensor_reduce(mean, heads(PS[:, 5, :]), AX.X, ALU.add))
                    link(nc.vector.tensor_scalar(mean, mean, 1.0 / P, None, ALU.mult))
                    link(nc.vector.tensor_tensor(heads(cen), heads(PS[:, 5, :]), per_head(mean), ALU.subtract))
                    link(nc.vector.tensor_tensor(sq, cen, cen, ALU.mult))
                    nc.vector.tensor_reduce(var, heads(sq), AX.X, ALU.add).then_inc(r_var, 1)
                    v.wait_ge(r_rstd, 2 * (t + 1))
                    if t:
                        v.wait_ge(r_to, t)
                    nc.vector.tensor_tensor(heads(on), heads(cen), per_head(rs), ALU.mult).then_inc(r_on, 1)

            @block.gpsimd
            def _(pool):
                var, rs = stat4[:, H:2 * H], stat4[:, 2 * H:3 * H]
                for t in range(NT):
                    pool.wait_ge(r_var, t + 1)
                    nc.gpsimd.tensor_scalar(rs, var, 1.0 / P, LN_EPS, ALU.mult, ALU.add).then_inc(r_rstd, 1)
                    pool.wait_ge(r_rstd, 2 * t + 1)
                    nc.gpsimd.tensor_tensor(rs, rs, nhalf[:, 0:H], ALU.pow).then_inc(r_rstd, 1)
                    pool.wait_ge(r_yt, t + 1)
                    pool.wait_ge(r_evA, 8)
                    ysl = yr[:, :, t * P:(t + 1) * P]
                    nc.gpsimd.tensor_tensor(ysl, heads(yt), ysl, ALU.mult).then_inc(r_y, 1)
        if dbg == "R":
            return

        region()
        PADS = SEQ + 4
        raw = carve(CH * PADS).rearrange("p (c s) -> p c s", c=CH)
        xc = carve(CH * SEQ).rearrange("p (c s) -> p c s", c=CH)
        yl = carve(CH * SEQ).rearrange("p (c s) -> p c s", c=CH)
        ring = [carve(KD * W).rearrange("p (k n) -> p k n", k=KD) for _ in range(2)]
        wri = carve(2 * CH * P).rearrange("p (g c n) -> p g c n", g=2, c=CH)
        rg = carve(CH * SEQ).rearrange("p (c s) -> p c s", c=CH)
        ig = carve(CH * SEQ).rearrange("p (c s) -> p c s", c=CH)
        th = [carve(SEQ) for _ in range(2)]
        sp_t = carve(8 * 32).rearrange("p (i n) -> p i n", i=8)
        lam8, nlam8 = carve(CH), carve(CH)
        l_w = [sem("l_w0"), sem("l_w1")]
        (l_par, l_grp, l_job, l_ev, l_chain, l_z, l_exp, l_lam, l_xc, l_gate, l_gev, l_mz, l_th, l_a, l_in, l_sq,
         l_y, l_st, l_pool) = (sem("l_" + n) for n in (
             "par", "grp", "job", "ev", "chain", "z", "exp", "lam", "xc", "gate", "gev", "mz", "th", "a", "in", "sq",
             "y", "st", "pool"))

        def softplus_start(v, link, z, tmp, n, out_sem):
            link(nc.vector.tensor_scalar(tmp[:, 0, 0:n], z, -1.0, None, ALU.mult))
            nc.vector.tensor_tensor(tmp[:, 0, 0:n], tmp[:, 0, 0:n], z, ALU.min).then_inc(out_sem, 1)

        def softplus_end(link, z, tmp, n):
            e, w, w2, q = (tmp[:, i, 0:n] for i in (1, 2, 3, 4))
            link(nc.vector.tensor_scalar(w, e, 2.0, None, ALU.add))
            link(nc.vector.reciprocal(w, w))
            link(nc.vector.tensor_tensor(w, w, e, ALU.mult))
            link(nc.vector.tensor_tensor(w2, w, w, ALU.mult))
            link(nc.vector.tensor_scalar(q, w2, 1.0 / 17, None, ALU.mult))
            for c in (15, 13, 11, 9, 7, 5, 3):
                link(nc.vector.scalar_tensor_tensor(q, q, 1.0 / c, w2, ALU.add, ALU.mult))
            link(nc.vector.scalar_tensor_tensor(q, q, 1.0, w, ALU.add, ALU.mult))
            link(nc.vector.tensor_scalar(q, q, 2.0, None, ALU.mult))
            link(nc.vector.scalar_tensor_tensor(q, z, 0.0, q, ALU.max, ALU.add))
            return q

        with nc.Block() as block:
            @block.sync
            def _(sp):
                for g, c0 in enumerate((C_LX, C_LG)):
                    sp.dma_start(ring[g], w_cols(c0, W)).then_inc(l_w[g], 16)
                sp.wait_ge(l_mz, 1)
                for g, name in enumerate(("lru_w_r", "lru_w_i")):
                    wv = a[name].rearrange("(c b) i j -> b i c j", b=2)
                    for b in range(2):
                        sp.dma_start(wri[b * 64:(b + 1) * 64, g, :, b * 64:(b + 1) * 64], wv[b]).then_inc(l_par, 16)
                sp.wait_ge(l_y, CH)
                sp.dma_start(y_d["lru"], yl).then_inc(l_st, 16)
                sp.wait_ge(l_st, 16)

            @block.tensor
            def _(pe):
                for g in range(2):
                    pe.wait_ge(l_w[g], 16)
                    for j in range(8):
                        job = 8 * g + j
                        if job >= 2:
                            pe.wait_ge(l_ev, job - 1)
                        project_channels(pe, ring[g], job % 2, j // 2, j % 2).then_inc(l_job, 1)
                pe.wait_ge(l_par, 64)
                n = 0
                for c in range(CH):
                    pe.wait_ge(l_xc, c + 1)
                    for g in range(2):
                        for half in range(2):
                            if n >= 4:
                                pe.wait_ge(l_gev, n - 3)
                            nc.tensor.matmul(PS[:, 2 + n % 4, :], wri[:, g, c, :], xc[:, c, half * HALF:(half + 1) * HALF],
                                             start=True, stop=True).then_inc(l_gate, 1)
                            n += 1

            @block.scalar
            def _(act):
                act.wait_ge(l_z, 1)
                nc.scalar.activation(sp_t[:, 1, 0:CH], sp_t[:, 0, 0:CH], ACT.Exp).then_inc(l_exp, 1)
                for job in range(16):
                    g, j = job // 8, job % 8
                    act.wait_ge(l_job, job + 1)
                    if g == 0:
                        nc.scalar.activation(raw[:, j // 2, 3 + (j % 2) * HALF:3 + (j % 2 + 1) * HALF], PS[:, job % 2, :],
                                             ACT.Identity, bias=col("b_lx", j // 2)).then_inc(l_ev, 1)
                    else:
                        nc.scalar.activation(yl[:, j // 2, (j % 2) * HALF:(j % 2 + 1) * HALF], PS[:, job % 2, :],
                                             ACT.Gelu_apprx_tanh, bias=col("b_lg", j // 2)).then_inc(l_ev, 1)
                n = 0
                for c in range(CH):
                    for g in range(2):
                        for half in range(2):
                            act.wait_ge(l_gate, n + 1)
                            nc.scalar.activation((rg, ig)[g][:, c, half * HALF:(half + 1) * HALF], PS[:, 2 + n % 4, :],
                                                 ACT.Sigmoid, bias=col(("lru_br", "lru_bi")[g], c)).then_inc(l_gev, 1)
                            n += 1
                act.wait_ge(l_gev, 16)
                act.wait_ge(l_lam, 1)
                for c in range(CH):
                    if c >= 2:
                        act.wait_ge(l_in, c - 1)
                    nc.scalar.activation(th[c % 2], rg[:, c, :], ACT.Tanh, scale=nlam8[:, c:c + 1]).then_inc(l_th, 1)
                    act.wait_ge(l_th, c + 1)
                    nc.scalar.activation(rg[:, c, :], rg[:, c, :], ACT.Exp, scale=lam8[:, c:c + 1]).then_inc(l_a, 1)
                for c in range(CH):
                    act.wait_ge(l_in, c + 1)
                    nc.scalar.activation(raw[:, c, 0:SEQ], raw[:, c, 0:SEQ], ACT.Sqrt).then_inc(l_sq, 1)

            @block.vector
            def _(v):
                link = chained(v, l_chain)
                lam = sp_t[:, 7, 0:CH]
                link(nc.vector.tensor_scalar(lam, col("lru_lam", 0, CH), -1.0, None, ALU.mult))
                softplus_start(v, link, lam, sp_t, CH, l_z)
                for g in range(2):
                    nc.vector.memset(wri[:, g, :, :], 0.0)
                for c in range(CH):
                    last = nc.vector.memset(raw[:, c, 0:3], 0.0)
                link(last)
                nc.vector.memset(sp_t[:, 6, 0:1], 0.0).then_inc(l_mz, 1)
                v.wait_ge(l_exp, 1)
                sp_lam = softplus_end(link, lam, sp_t, CH)
                link(nc.vector.tensor_scalar(lam8, sp_lam, -LRU_C, None, ALU.mult))
                nc.vector.tensor_scalar(nlam8, sp_lam, LRU_C, None, ALU.mult).then_inc(l_lam, 1)
                for c in range(CH):
                    v.wait_ge(l_ev, 2 * c + 2)
                    tap = [col("lru_w", 4 * j + c) for j in range(4)]
                    link(nc.vector.tensor_scalar(xc[:, c, :], raw[:, c, 3:3 + SEQ], tap[3], col("lru_cb", c),
                                                 ALU.mult, ALU.add))
                    for j in range(3):
                        ins = nc.vector.scalar_tensor_tensor(xc[:, c, :], raw[:, c, j:j + SEQ], tap[j], xc[:, c, :],
                                                             ALU.mult, ALU.add)
                        if j < 2:
                            link(ins)
                    ins.then_inc(l_xc, 1)
                v.wait_ge(l_xc, CH)
                for c in range(CH):
                    v.wait_ge(l_a, c + 1)
                    link(nc.vector.tensor_tensor(raw[:, c, 0:SEQ], rg[:, c, :], rg[:, c, :], ALU.mult))
                    nc.vector.scalar_tensor_tensor(raw[:, c, 0:SEQ], raw[:, c, 0:SEQ], 1.0, th[c % 2],
                                                   ALU.add, ALU.mult).then_inc(l_in, 1)
                for c in range(CH):
                    v.wait_ge(l_sq, c + 1)
                    link(nc.vector.tensor_tensor(ig[:, c, :], ig[:, c, :], xc[:, c, :], ALU.mult))
                    link(nc.vector.tensor_tensor(ig[:, c, :], ig[:, c, :], raw[:, c, 0:SEQ], ALU.mult))
                    link(nc.vector.tensor_tensor_scan(xc[:, c, :], rg[:, c, :], ig[:, c, :], 0.0, ALU.mult, ALU.add))
                    nc.vector.tensor_tensor(yl[:, c, :], yl[:, c, :], xc[:, c, :], ALU.mult).then_inc(l_y, 1)
        if dbg == "L":
            return

        region()
        QT = 3 * CH
        raw = carve(QT * PADS).rearrange("p (c s) -> p c s", c=QT)
        kn, vn, X, Xt, yg = (carve(NT * W) for _ in range(5))
        ring = [x.rearrange("p (k n) -> p k n", k=KD) for x in (X, Xt)]
        kn, vn, X, Xt = (tok3(x) for x in (kn, vn, X, Xt))
        yg = yg.rearrange("p (c s) -> p c s", c=CH)
        mark = top[0]
        ctmp = [carve(SEQ) for _ in range(2)]
        top[0] = mark
        qk, sqk = carve(2 * W), carve(2 * W)
        qn, qd, kb, qT, kT, kbT, E = (carve(W) for _ in range(7))
        top2 = top[0]
        top[0] = mark
        Bt = [carve(W) for _ in range(2)]
        Pm = [carve(W) for _ in range(2)]
        kbg, vb, kd, nwT, vnew, sq, on = (carve(W) for _ in range(7))
        top[0] = max(top[0], top2)
        S = [carve(W) for _ in range(2)]
        ones = carve(P)
        wba = carve(KD * 2 * H).rearrange("p (k n) -> p k n", k=KD)
        gba = carve(NT * 2 * H).rearrange("p (t n) -> p t n", t=NT)
        small = carve(10 * 32).rearrange("p (i n) -> p i n", i=10)
        sp_t = carve(8 * 32).rearrange("p (i n) -> p i n", i=8)
        z, la, beta, gcC, gl, egc, egl, kdf, bg = (small[:, i, :] for i in range(9))
        rows8 = carve(8 + 3 * H)
        b_ba, b_dt, b_al, nea = rows8[:, 0:8], rows8[:, 8:12], rows8[:, 12:16], rows8[:, 16:20]
        rn, ss = carve(2 * H), carve(2 * H)
        g_w = [sem("g_w0"), sem("g_w1")]
        G_GROUPS = (C_QKV, C_QKV + W, C_QKV + 2 * W, C_GG)
        (g_par, g_grp, g_job, g_ev, g_chain, g_cv, g_si, g_ba, g_bae, g_sm, g_act, g_cum, g_cume, g_fac, g_tqk, g_tv,
         g_cqk, g_cv3, g_ss, g_rn, g_prep, g_t4, g_c4, g_kk, g_gb, g_E, g_Ee, g_at, g_one) = (sem("g_" + n) for n in (
             "par", "grp", "job", "ev", "chain", "cv", "si", "ba", "bae", "sm", "act", "cum", "cume", "fac", "tqk", "tv",
             "cqk", "cv3", "ss", "rn", "prep", "t4", "c4", "kk", "gb", "E", "Ee", "at", "one"))
        (g_B, g_P, g_Pc, g_U, g_X, g_pre, g_wT, g_wTc, g_vn, g_vnc, g_o, g_dS, g_S, g_sq, g_var, g_rs, g_on, g_to,
         g_y, g_st) = (sem("g2_" + n) for n in (
             "B", "P", "Pc", "U", "X", "pre", "wT", "wTc", "vn", "vnc", "o", "dS", "S", "sq", "var", "rs", "on", "to",
             "y", "st"))

        def hd(ap, hh):
            return ap[:, hh * P:(hh + 1) * P]

        def tile4(ap, t):
            return ap[:, :, t * P:(t + 1) * P]

        def fac(f, t):
            return per_head(f[:, t * H:(t + 1) * H])

        with nc.Block() as block:
            @block.sync
            def _(sp):
                sp.dma_start(wba, w_in[:, C_BA:C_BA + 2 * H].rearrange("(k p) n -> p k n", p=P)).then_inc(g_par, 16)
                sp.dma_start(b_ba, row("b_in", C_BA, 2 * H)).then_inc(g_par, 16)
                sp.dma_start(b_dt, row("gdn_dt_bias", 0, H)).then_inc(g_par, 16)
                sp.dma_start(b_al, row("gdn_a_log", 0, H)).then_inc(g_par, 16)
                for g, c0 in enumerate(G_GROUPS):
                    if g >= 2:
                        sp.wait_ge(g_grp, g - 1)
                    sp.dma_start(ring[g % 2], w_cols(c0, W)).then_inc(g_w[g % 2], 16)
                sp.wait_ge(g_y, NT)
                sp.dma_start(y_d["gdn"], yg).then_inc(g_st, 16)
                sp.wait_ge(g_st, 16)

            @block.tensor
            def _(pe):
                pe.wait_ge(g_par, 64)
                for t in range(NT):
                    for k in range(KD):
                        last = nc.tensor.matmul(PS[:, 2, t * 8:(t + 1) * 8], hT[:, k, t * P:(t + 1) * P], wba[:, k, :],
                                                start=(k == 0), stop=(k == KD - 1))
                last.then_inc(g_ba, 1)
                for g in range(4):
                    pe.wait_ge(g_w[g % 2], 16 * (g // 2 + 1))
                    for j in range(8):
                        job = 8 * g + j
                        if job >= 2:
                            pe.wait_ge(g_ev, job - 1)
                        project_channels(pe, ring[g % 2], job % 2, j // 2, j % 2).then_inc(g_job, 1)
                    pe.wait_ge(g_job, 8 * (g + 1))
                    pe.sem_inc(g_grp, 1)
                pe.wait_ge(g_sm, 1)
                pe.wait_ge(g_one, 1)
                nc.tensor.matmul(PS[:, 3, 0:32], upper, la, start=True, stop=True)
                nc.tensor.matmul(PS[:, 3, 32:64], ones, la, start=True, stop=True).then_inc(g_cum, 1)
                pe.wait_ge(g_fac, 1)
                pe.wait_ge(g_si, QT)
                pe.wait_ge(g_ev, 32)
                for t in range(NT):
                    if t:
                        pe.wait_ge(g_cqk, t)
                    for i in range(2 * H):
                        last = nc.tensor.transpose(PS[:, 2 + i // 4, (i % 4) * P:(i % 4 + 1) * P],
                                                   raw[:, i, t * P:(t + 1) * P], ident)
                    last.then_inc(g_tqk, 1)
                    if t:
                        pe.wait_ge(g_Ee, t)
                    for i in range(H):
                        last = nc.tensor.transpose(PS[:, 4, i * P:(i + 1) * P], raw[:, 8 + i, t * P:(t + 1) * P], ident)
                    last.then_inc(g_tv, 1)
                    pe.wait_ge(g_prep, t + 1)
                    if t:
                        pe.wait_ge(g_at, t)
                    for bank, src in ((5, qn), (6, qd), (0, kb)):
                        for hh in range(H):
                            last = nc.tensor.transpose(hd(PS[:, bank, :], hh), hd(src, hh), ident)
                    for hh in range(H):
                        last = nc.tensor.transpose(hd(PS[:, 7, :], hh), hd(kn[:, t, :], hh), ident)
                    last.then_inc(g_t4, 1)
                    pe.wait_ge(g_cv3, t + 1)
                    for hh in range(H):
                        last = nc.tensor.matmul(hd(PS[:, 4, :], hh), la[:, t * H + hh:t * H + hh + 1].broadcast_to([P, P]),
                                                upper, start=True, stop=True)
                    last.then_inc(g_gb, 1)
                    pe.wait_ge(g_c4, 4 * (t + 1))
                    for hh in range(H):
                        nc.tensor.matmul(hd(PS[:, 1, :], hh), hd(kT, hh), hd(kbT, hh), start=True, stop=True)
                    for hh in range(H):
                        last = nc.tensor.matmul(hd(PS[:, 5, :], hh), hd(kT, hh), hd(qT, hh), start=True, stop=True)
                    last.then_inc(g_kk, 1)
                n_i = LEVELS * NT

                def product(i):
                    t = i % NT
                    pe.wait_ge(g_B, i + 1)
                    if i >= 2:
                        pe.wait_ge(g_Pc, i - 1)
                    if i >= NT:
                        pe.wait_ge(g_X, i - NT + 1)
                    for hh in range(H):
                        last = nc.tensor.matmul(hd(PS[:, 2 + i % 2, :], hh), hd(Bt[i % 2], hh), hd(X[:, t, :], hh),
                                                start=True, stop=True)
                    last.then_inc(g_P, 1)

                def update(i):
                    t = i % NT
                    pe.wait_ge(g_Pc, i + 1)
                    if i >= 2:
                        pe.wait_ge(g_X, i - 1)
                    if i // NT < LEVELS - 1:
                        for hh in range(H):
                            nc.tensor.matmul(hd(PS[:, 4 + i % 2, :], hh), hd(Xt[:, t, :], hh), hd(Pm[i % 2], hh),
                                             start=True, stop=True)
                    for hh in range(H):
                        last = nc.tensor.matmul(hd(PS[:, 6 + i % 2, :], hh), hd(Pm[i % 2], hh), hd(Xt[:, t, :], hh),
                                                start=True, stop=True)
                    last.then_inc(g_U, 1)

                pe.wait_ge(g_at, NT)
                for i in range(n_i):
                    product(i)
                    if i:
                        update(i - 1)
                update(n_i - 1)
                pe.wait_ge(g_X, n_i)
                for t in range(NT):
                    pe.wait_ge(g_pre, t + 1)
                    if t:
                        pe.wait_ge(g_wTc, t)
                    for hh in range(H):
                        last = nc.tensor.matmul(hd(PS[:, 2, :], hh), hd(kbg, hh), hd(Xt[:, t, :], hh), start=True, stop=True)
                    last.then_inc(g_wT, 1)
                    if t:
                        pe.wait_ge(g_wTc, t + 1)
                        pe.wait_ge(g_S, t)
                        pe.wait_ge(g_vnc, t)
                    for hh in range(H):
                        last = nc.tensor.matmul(hd(PS[:, 3, :], hh), hd(Xt[:, t, :], hh), hd(vb, hh), start=True, stop=(t == 0))
                        if t:
                            last = nc.tensor.matmul(hd(PS[:, 3, :], hh), hd(nwT, hh), hd(S[t % 2], hh), start=False, stop=True)
                    last.then_inc(g_vn, 1)
                    pe.wait_ge(g_vnc, t + 1)
                    for hh in range(H):
                        last = nc.tensor.matmul(hd(PS[:, 5, :], hh), hd(kd, hh), hd(vnew, hh), start=True, stop=True)
                    last.then_inc(g_dS, 1)
                    if t:
                        pe.wait_ge(g_on, t)
                    for hh in range(H):
                        last = nc.tensor.matmul(hd(PS[:, 4, :], hh), raw[:, 8 + hh, t * P:(t + 1) * P], hd(vnew, hh),
                                                start=True, stop=(t == 0))
                        if t:
                            last = nc.tensor.matmul(hd(PS[:, 4, :], hh), raw[:, hh, t * P:(t + 1) * P], hd(S[t % 2], hh),
                                                    start=False, stop=True)
                    last.then_inc(g_o, 1)
                    pe.wait_ge(g_on, t + 1)
                    if t:
                        pe.wait_ge(g_y, t)
                    for hh in range(H):
                        last = nc.tensor.transpose(hd(PS[:, 6, :], hh), hd(on, hh), ident)
                    last.then_inc(g_to, 1)

            @block.scalar
            def _(act):
                def silu(c):
                    act.wait_ge(g_cv, c + 1)
                    nc.scalar.activation(raw[:, c, 0:SEQ], ctmp[c % 2], ACT.Silu).then_inc(g_si, 1)

                for job in range(32):
                    c, half = job // 2, job % 2
                    act.wait_ge(g_job, job + 1)
                    if job < 24:
                        nc.scalar.activation(raw[:, c, 3 + half * HALF:3 + (half + 1) * HALF], PS[:, job % 2, :],
                                             ACT.Identity, bias=col("b_qkv", c)).then_inc(g_ev, 1)
                    else:
                        nc.scalar.activation(yg[:, c - QT, half * HALF:(half + 1) * HALF], PS[:, job % 2, :],
                                             ACT.Silu, bias=col("b_gg", c - QT)).then_inc(g_ev, 1)
                    if half and 1 <= c <= QT:
                        silu(c - 1)
                act.wait_ge(g_bae, 1)
                nc.scalar.activation(beta.rearrange("p (t n) -> p t n", t=NT), gba[:, :, 0:H], ACT.Sigmoid).then_inc(g_act, 1)
                nc.scalar.activation(sp_t[:, 1, :], sp_t[:, 0, :], ACT.Exp).then_inc(g_act, 1)
                nc.scalar.activation(nea, b_al, ACT.Exp).then_inc(g_act, 1)
                act.wait_ge(g_cume, 1)
                nc.scalar.activation(egc, gcC, ACT.Exp).then_inc(g_act, 1)
                nc.scalar.activation(egl, gl, ACT.Exp).then_inc(g_act, 1)
                nc.scalar.activation(kdf, kdf, ACT.Exp).then_inc(g_act, 1)
                for t in range(NT):
                    act.wait_ge(g_tqk, t + 1)
                    if t:
                        act.wait_ge(g_prep, t)
                    nc.scalar.activation(qk.rearrange("p (b n) -> p b n", b=2), PS[:, 2:4, :], ACT.Copy).then_inc(g_cqk, 1)
                    act.wait_ge(g_tv, t + 1)
                    nc.scalar.activation(vn[:, t, :], PS[:, 4, :], ACT.Copy).then_inc(g_cv3, 1)
                    act.wait_ge(g_t4, t + 1)
                    if t:
                        act.wait_ge(g_kk, t)
                    nc.scalar.activation(qT, PS[:, 5, :], ACT.Copy).then_inc(g_c4, 1)
                    nc.scalar.activation(kT, PS[:, 7, :], ACT.Copy).then_inc(g_c4, 1)
                    nc.scalar.activation(kbT, PS[:, 0, :], ACT.Copy).then_inc(g_c4, 1)
                    nc.scalar.activation(tile4(raw[:, 0:4, :], t), heads(PS[:, 6, :]), ACT.Copy).then_inc(g_c4, 1)
                    act.wait_ge(g_E, t + 1)
                    nc.scalar.activation(E, E, ACT.Exp).then_inc(g_Ee, 1)
                for i in range(LEVELS * NT):
                    act.wait_ge(g_P, i + 1)
                    if i >= 2:
                        act.wait_ge(g_U, i - 1)
                    nc.scalar.activation(Pm[i % 2], PS[:, 2 + i % 2, :], ACT.Copy).then_inc(g_Pc, 1)
                for t in range(NT):
                    act.wait_ge(g_wT, t + 1)
                    if t:
                        act.wait_ge(g_vn, t)
                    nc.scalar.activation(nwT, PS[:, 2, :], ACT.Copy, scale=-1.0).then_inc(g_wTc, 1)
                    act.wait_ge(g_o, t + 1)
                    if t:
                        act.wait_ge(g_var, t)
                    nc.scalar.activation(sq, PS[:, 4, :], ACT.Square).then_inc(g_sq, 1)

            @block.vector
            def _(v):
                link = chained(v, g_chain)
                for c in range(QT):
                    nc.vector.memset(raw[:, c, 0:3], 0.0)
                nc.vector.memset(ones, 1.0).then_inc(g_one, 1)
                v.wait_ge(g_one, 1)
                v.wait_ge(g_ba, 1)
                v.wait_ge(g_par, 64)
                link(nc.vector.tensor_tensor(gba, PS[:, 2, 0:64].rearrange("p (t n) -> p t n", t=NT),
                                             b_ba.unsqueeze(1).broadcast_to([P, NT, 8]), ALU.add))
                link(nc.vector.tensor_tensor(z.rearrange("p (t n) -> p t n", t=NT), gba[:, :, H:2 * H],
                                             b_dt.unsqueeze(1).broadcast_to([P, NT, H]), ALU.add))
                softplus_start(v, link, z, sp_t, 32, g_bae)
                for c in range(QT):
                    v.wait_ge(g_ev, 2 * c + 2)
                    if c >= 2:
                        v.wait_ge(g_si, c - 1)
                    tap = [col("gdn_w", QT * j + c) for j in range(4)]
                    dst = ctmp[c % 2]
                    link(nc.vector.tensor_scalar(dst, raw[:, c, 3:3 + SEQ], tap[3], None, ALU.mult))
                    for j in range(3):
                        ins = nc.vector.scalar_tensor_tensor(dst, raw[:, c, j:j + SEQ], tap[j], dst, ALU.mult, ALU.add)
                        if j < 2:
                            link(ins)
                    ins.then_inc(g_cv, 1)
                v.wait_ge(g_act, 3)
                sp_z = softplus_end(link, z, sp_t, 32)
                link(nc.vector.tensor_scalar(nea, nea, -1.0, None, ALU.mult))
                nc.vector.tensor_tensor(la.rearrange("p (t n) -> p t n", t=NT), sp_z.rearrange("p (t n) -> p t n", t=NT),
                                        nea.unsqueeze(1).broadcast_to([P, NT, H]), ALU.mult).then_inc(g_sm, 1)
                v.wait_ge(g_cum, 1)
                link(nc.vector.tensor_copy(gcC, PS[:, 3, 0:32]))
                link(nc.vector.tensor_copy(gl, PS[:, 3, 32:64]))
                nc.vector.tensor_tensor(kdf, gl, gcC, ALU.subtract).then_inc(g_cume, 1)
                v.wait_ge(g_act, 6)
                nc.vector.tensor_tensor(bg, beta, egc, ALU.mult).then_inc(g_fac, 1)
                v.wait_ge(g_fac, 1)
                for t in range(NT):
                    v.wait_ge(g_cqk, t + 1)
                    link(nc.vector.tensor_tensor(sqk, qk, qk, ALU.mult))
                    nc.vector.tensor_reduce(ss, sqk.rearrange("p (h c) -> p h c", h=2 * H), AX.X, ALU.add).then_inc(g_ss, 1)
                    v.wait_ge(g_rn, 3 * (t + 1))
                    if t:
                        v.wait_ge(g_t4, t)
                    link(nc.vector.tensor_tensor(heads(qn), heads(qk[:, 0:W]), per_head(rn[:, 0:H]), ALU.mult))
                    link(nc.vector.tensor_tensor(heads(kn[:, t, :]), heads(qk[:, W:2 * W]), per_head(rn[:, H:2 * H]), ALU.mult))
                    link(nc.vector.tensor_tensor(heads(qd), heads(qn), fac(egc, t), ALU.mult))
                    nc.vector.tensor_tensor(heads(kb), heads(kn[:, t, :]), fac(beta, t), ALU.mult).then_inc(g_prep, 1)
                    v.wait_ge(g_gb, t + 1)
                    for hh in range(H):
                        last = nc.vector.tensor_scalar(hd(E, hh), hd(PS[:, 4, :], hh), gcC[:, t * H + hh:t * H + hh + 1], 0.0,
                                                       ALU.subtract, ALU.min)
                    last.then_inc(g_E, 1)
                    v.wait_ge(g_Ee, t + 1)
                    link(nc.vector.tensor_tensor(heads(E), heads(E), upper.unsqueeze(1).broadcast_to([P, H, P]), ALU.mult))
                    v.wait_ge(g_kk, t + 1)
                    nc.vector.tensor_tensor(tile4(raw[:, 4:8, :], t), heads(PS[:, 1, :]), heads(E), ALU.mult)
                    nc.vector.tensor_tensor(tile4(raw[:, 8:12, :], t), heads(PS[:, 5, :]), heads(E), ALU.mult).then_inc(g_at, 1)
                v.wait_ge(g_at, NT)
                v.wait_ge(g_kk, NT)
                eye4 = ident.unsqueeze(1).broadcast_to([P, H, P])
                for t in range(NT):
                    nc.vector.tensor_copy(heads(X[:, t, :]), eye4)
                    last = nc.vector.tensor_copy(heads(Xt[:, t, :]), eye4)
                link(last)

                def level_block(i):
                    s, t = i // NT, i % NT
                    if i >= 2:
                        v.wait_ge(g_P, i - 1)
                    mask = const("level")[:, s * P:(s + 1) * P].unsqueeze(1).broadcast_to([P, H, P])
                    nc.vector.tensor_tensor(heads(Bt[i % 2]), tile4(raw[:, 4:8, :], t), mask, ALU.mult).then_inc(g_B, 1)

                n_i = LEVELS * NT
                level_block(0)
                for i in range(n_i):
                    s, t = i // NT, i % NT
                    if i + 1 < n_i:
                        level_block(i + 1)
                    v.wait_ge(g_U, i + 1)
                    if s < LEVELS - 1:
                        nc.vector.tensor_tensor(X[:, t, :], X[:, t, :], PS[:, 4 + i % 2, :], ALU.subtract)
                    nc.vector.tensor_tensor(Xt[:, t, :], Xt[:, t, :], PS[:, 6 + i % 2, :], ALU.subtract).then_inc(g_X, 1)
                for t in range(NT):
                    if t:
                        v.wait_ge(g_dS, t)
                        v.wait_ge(g_vn, t)
                    nc.vector.tensor_tensor(heads(kbg), heads(kn[:, t, :]), fac(bg, t), ALU.mult)
                    nc.vector.tensor_tensor(heads(vb), heads(vn[:, t, :]), fac(beta, t), ALU.mult)
                    nc.vector.tensor_tensor(heads(kd), heads(kn[:, t, :]), fac(kdf, t), ALU.mult).then_inc(g_pre, 1)
                    v.wait_ge(g_vn, t + 1)
                    if t:
                        v.wait_ge(g_o, t)
                    nc.vector.tensor_copy(vnew, PS[:, 3, :]).then_inc(g_vnc, 1)
                    v.wait_ge(g_dS, t + 1)
                    for hh in range(H):
                        if t == 0:
                            last = nc.vector.tensor_copy(hd(S[1], hh), hd(PS[:, 5, :], hh))
                        else:
                            last = nc.vector.scalar_tensor_tensor(hd(S[(t + 1) % 2], hh), hd(S[t % 2], hh),
                                                                  egl[:, t * H + hh:t * H + hh + 1], hd(PS[:, 5, :], hh),
                                                                  ALU.mult, ALU.add)
                    last.then_inc(g_S, 1)
                    v.wait_ge(g_S, t + 1)
                    v.wait_ge(g_sq, t + 1)
                    nc.vector.tensor_reduce(ss[:, 0:H], heads(sq), AX.X, ALU.add).then_inc(g_var, 1)
                    v.wait_ge(g_rs, 2 * (t + 1))
                    if t:
                        v.wait_ge(g_to, t)
                    nc.vector.tensor_tensor(heads(on), heads(PS[:, 4, :]), per_head(rn[:, 0:H]), ALU.mult).then_inc(g_on, 1)
                    v.wait_ge(g_to, t + 1)
                    nc.vector.scalar_tensor_tensor(tile4(yg, t), heads(PS[:, 6, :]), col("gdn_g", 0), tile4(yg, t),
                                                   ALU.mult, ALU.mult).then_inc(g_y, 1)

            @block.gpsimd
            def _(pool):
                for t in range(NT):
                    pool.wait_ge(g_ss, t + 1)
                    nc.gpsimd.tensor_scalar(rn, ss, 1e-6, None, ALU.add).then_inc(g_rn, 1)
                    pool.wait_ge(g_rn, 3 * t + 1)
                    nc.gpsimd.tensor_tensor(rn, rn, nhalf[:, 0:2 * H], ALU.pow).then_inc(g_rn, 1)
                    pool.wait_ge(g_rn, 3 * t + 2)
                    nc.gpsimd.tensor_scalar(rn[:, 0:H], rn[:, 0:H], float(P) ** -0.5, None, ALU.mult).then_inc(g_rn, 1)
                for t in range(NT):
                    pool.wait_ge(g_var, t + 1)
                    nc.gpsimd.tensor_scalar(rn[:, 0:H], ss[:, 0:H], 1.0 / P, 1e-6, ALU.mult, ALU.add).then_inc(g_rs, 1)
                    pool.wait_ge(g_rs, 2 * t + 1)
                    nc.gpsimd.tensor_tensor(rn[:, 0:H], rn[:, 0:H], nhalf[:, 0:H], ALU.pow).then_inc(g_rs, 1)
        if dbg == "G":
            return

        region()
        mT = carve(KD * SEQ).rearrange("p (k s) -> p k s", k=KD)
        after_mT = top[0]
        ys = [carve(CH * SEQ).rearrange("p (c s) -> p c s", c=CH) for _ in range(3)]
        wm = [carve(KD * 3 * P).rearrange("p (k n c) -> p k n c", k=KD, n=3) for _ in range(2)]
        wb = [carve(CH * 3 * P).rearrange("p (k n c) -> p k n c", k=CH, n=3) for _ in range(2)]
        sg = [carve(HALF) for _ in range(2)]
        prod = [carve(HALF) for _ in range(2)]
        m_y, m_w = sem("m_y"), [sem("m_w0"), sem("m_w1")]
        m_read, m_g, m_b, m_sg, m_acc, m_chain = (sem("m_" + n) for n in ("read", "gate", "branch", "sg", "acc", "chain"))
        wmg_v = [w_in[:, C_MG + n * D:C_MG + (n + 1) * D].rearrange("(k p) c -> p k c", p=P) for n in range(3)]
        wbr_v = [a["w_branch"][n].rearrange("(k p) c -> p k c", p=P) for n in range(3)]
        PER = 6
        with nc.Block() as block:
            @block.sync
            def _(sp):
                for n, name in enumerate(("ret", "gdn", "lru")):
                    sp.dma_start(ys[n], y_d[name]).then_inc(m_y, 16)
                with sp.Fori(0, KD // 2) as i:
                    for u in range(2):
                        dt = 2 * i + u
                        sp.wait_ge(m_read, dt + 1)
                        for n in range(3):
                            sp.dma_start(wm[u][:, :, n, :], wmg_v[n][:, :, bass.ds(dt * P, P)]).then_inc(m_w[u], 16)
                            sp.dma_start(wb[u][:, :, n, :], wbr_v[n][:, :, bass.ds(dt * P, P)]).then_inc(m_w[u], 16)

            @block.tensor
            def _(pe):
                pe.sem_inc(m_read, 2)
                pe.wait_ge(m_y, 48)
                with pe.Fori(0, KD // 2) as i:
                    for u in range(2):
                        pe.wait_ge(m_w[u], 96 * i + 96)
                        for q in range(PER):
                            half, n = q // 3, q % 3
                            item = 12 * i + PER * u + q
                            b = 2 * ((PER * u + q) % 4)
                            hs = slice(half * HALF, (half + 1) * HALF)
                            pe.wait_ge(m_acc, item + 1)
                            for k in range(KD):
                                last = nc.tensor.matmul(PS[:, b, :], wm[u][:, k, n, :], hT[:, k, hs],
                                                        start=(k == 0), stop=(k == KD - 1))
                            last.then_inc(m_g, 1)
                            for k in range(CH):
                                last = nc.tensor.matmul(PS[:, b + 1, :], wb[u][:, k, n, :], ys[n][:, k, hs],
                                                        start=(k == 0), stop=(k == CH - 1))
                            last.then_inc(m_b, 1)
                        pe.wait_ge(m_b, 12 * i + PER * (u + 1))
                        pe.sem_inc(m_read, 1)

            @block.scalar
            def _(act):
                for item in range(KD * PER):
                    dt, n = item // PER, item % 3
                    act.wait_ge(m_g, item + 1)
                    act.wait_ge(m_acc, item + 3)
                    nc.scalar.activation(sg[item % 2], PS[:, 2 * (item % 4), :], ACT.Sigmoid,
                                         bias=col("b_mg", n * KD + dt)).then_inc(m_sg, 1)

            @block.vector
            def _(v):
                v.sem_inc(m_acc, 4)
                with v.Fori(0, KD // 2) as i:
                    for u in range(2):
                        for q in range(PER):
                            half, n = q // 3, q % 3
                            item = 12 * i + PER * u + q
                            b = 2 * ((PER * u + q) % 4) + 1
                            v.wait_ge(m_sg, item + 1)
                            v.wait_ge(m_b, item + 1)
                            dst = mT[:, bass.ds(2 * i + u, 1), half * HALF:(half + 1) * HALF].rearrange("p a s -> p (a s)")
                            if n == 0:
                                nc.vector.tensor_tensor(dst, PS[:, b, :], sg[q % 2], ALU.mult).then_inc(m_acc, 1)
                            else:
                                nc.vector.tensor_tensor(prod[q % 2], PS[:, b, :], sg[q % 2], ALU.mult).then_inc(m_chain, 1)
                                v.wait_ge(m_acc, item + 4)
                                v.wait_ge(m_chain, 8 * i + 4 * u + 2 * half + n)
                                nc.vector.tensor_tensor(dst, dst, prod[q % 2], ALU.add).then_inc(m_acc, 1)

        top[0] = after_mT
        h = tok3(carve(NT * D))
        wo = carve(KD * D).rearrange("p (k n) -> p k n", k=KD)
        g_row, b_row = carve(D), carve(D)
        st = carve(NT * 12).rearrange("p (t j s) -> p t j s", t=NT, j=2)
        mv = carve(NT * 2).rearrange("p (t s) -> p t s", t=NT)
        rstd = carve(NT)
        o_par, o_h, o_w = sem("o_params"), sem("o_h"), [sem("o_w0"), sem("o_w1")]
        o_job, o_res, o_chain, o_stat, o_rstd, o_n, o_tp, o_hT, o_st = (sem("o_" + n) for n in (
            "job", "res", "chain", "stat", "rstd", "norm", "tp", "hT", "st"))
        with nc.Block() as block:
            @block.sync
            def _(sp):
                wv = a["w_out"].rearrange("(k p) n -> p k n", p=P)
                for j in range(2):
                    sp.dma_start(wo[:, :, j * HALF:(j + 1) * HALF], wv[:, :, j * HALF:(j + 1) * HALF]).then_inc(o_w[j], 16)
                sp.dma_start(h, h_d).then_inc(o_h, 16)
                sp.dma_start(g_row, row("ln1_g", 0, D)).then_inc(o_par, 16)
                sp.dma_start(b_row, row("ln1_b", 0, D)).then_inc(o_par, 16)
                sp.wait_ge(o_n, NT)
                sp.dma_start(h_d, h).then_inc(o_st, 16)
                sp.wait_ge(o_st, 16)

            @block.tensor
            def _(pe):
                pe.wait_ge(o_w[0], 16)
                pe.wait_ge(o_w[1], 16)
                for job in range(2 * NT):
                    t, j = job // 2, job % 2
                    if job >= 4:
                        pe.wait_ge(o_res, job - 3)
                    for k in range(KD):
                        last = nc.tensor.matmul(PS[:, 4 + job % 4, :], mT[:, k, t * P:(t + 1) * P],
                                                wo[:, k, j * HALF:(j + 1) * HALF], start=(k == 0), stop=(k == KD - 1))
                    last.then_inc(o_job, 1)
                transpose_tiles(pe, h, o_n, o_tp, o_hT)

            @block.scalar
            def _(act):
                copy_transposed(act, hT, o_tp, o_hT)

            @block.vector
            def _(v):
                link = chained(v, o_chain)
                v.wait_ge(o_h, 16)
                for job in range(2 * NT):
                    t, j = job // 2, job % 2
                    v.wait_ge(o_job, job + 1)
                    hs = h[:, t, j * HALF:(j + 1) * HALF]
                    nc.vector.scalar_tensor_tensor(hs, hs, ALPHA, PS[:, 4 + job % 4, :], ALU.mult, ALU.add).then_inc(o_res, 1)
                    if j:
                        v.wait_ge(o_res, job + 1)
                        ln_stats(v, link, h, st, mv, t).then_inc(o_stat, 1)
                v.wait_ge(o_rstd, 2)
                v.wait_ge(o_par, 32)
                for t in range(NT):
                    ln_apply(link, h, t, mv, rstd, g_row, b_row).then_inc(o_n, 1)

            @block.gpsimd
            def _(pool):
                pool.wait_ge(o_stat, NT)
                nc.gpsimd.tensor_scalar(rstd, mv[:, :, 1], LN_EPS, None, ALU.add).then_inc(o_rstd, 1)
                pool.wait_ge(o_rstd, 1)
                nc.gpsimd.tensor_tensor(rstd, rstd, nhalf[:, 0:NT], ALU.pow).then_inc(o_rstd, 1)
        if dbg == "O":
            return

        end_stage()
        region()
        acc = tok3(carve(NT * D))
        after_acc = top[0]
        wr = carve(KD * NE).rearrange("p (k e) -> p k e", k=KD)
        rb = carve(NE)
        G = carve(NT * NE)
        after_G = top[0]
        sc, sel, rep = (carve(NT * NE) for _ in range(3))
        m8 = carve(NT * NG * 8)
        gsc, rank, gmask = (carve(NT * NG) for _ in range(3))
        cmp_, eqv, ltg = (carve(NT * NG * NG) for _ in range(3))
        t8 = carve(NT * 8)
        den = carve(NT)
        e_par, e_h, e_lg, e_sc, e_chain, e_cst, e_g, e_gd = (sem("e_" + n) for n in (
            "par", "h", "logits", "scores", "chain", "const", "gates", "gdram"))

        def v4(ap):
            return ap.rearrange("p (t g e) -> p t g e", t=NT, g=NG)

        with nc.Block() as block:
            @block.sync
            def _(sp):
                sp.dma_start(wr, a["router_w"].rearrange("(k p) e -> p k e", p=P)).then_inc(e_par, 16)
                sp.dma_start(rb, row("router_b", 0, NE)).then_inc(e_par, 16)
                sp.dma_start(ltg, a["before"].rearrange("(a n) -> a n", a=1).broadcast_to([P, NT * NG * NG])).then_inc(e_par, 16)
                sp.dma_start(acc, h_d).then_inc(e_h, 16)

            @block.tensor
            def _(pe):
                pe.wait_ge(e_par, 48)
                for t in range(NT):
                    for k in range(KD):
                        last = nc.tensor.matmul(PS[:, 0, t * NE:(t + 1) * NE], hT[:, k, t * P:(t + 1) * P], wr[:, k, :],
                                                start=(k == 0), stop=(k == KD - 1))
                last.then_inc(e_lg, 1)

            @block.scalar
            def _(act):
                act.wait_ge(e_lg, 1)
                nc.scalar.activation(sc, PS[:, 0, :], ACT.Sigmoid).then_inc(e_sc, 1)

            @block.vector
            def _(v):
                link = chained(v, e_chain)
                v.wait_ge(e_sc, 1)
                v.wait_ge(e_par, 48)
                s3 = sel.rearrange("p (t e) -> p t e", t=NT)
                link(nc.vector.tensor_tensor(s3, sc.rearrange("p (t e) -> p t e", t=NT),
                                             rb.unsqueeze(1).broadcast_to([P, NT, NE]), ALU.add))
                for i in range(NT * NG):
                    last = nc.vector.max(m8[:, i * 8:(i + 1) * 8], sel[:, i * 8:(i + 1) * 8])
                link(last)
                m3 = m8.rearrange("p (i e) -> p i e", e=8)
                link(nc.vector.tensor_tensor(gsc, m3[:, :, 0], m3[:, :, 1], ALU.add))
                g3 = gsc.rearrange("p (t g) -> p t g", t=NT)
                mine = g3.unsqueeze(3).broadcast_to([P, NT, NG, NG])
                other = g3.unsqueeze(2).broadcast_to([P, NT, NG, NG])
                nc.vector.tensor_tensor(v4(cmp_), other, mine, ALU.is_gt)
                link(nc.vector.tensor_tensor(v4(eqv), other, mine, ALU.is_equal))
                link(nc.vector.tensor_tensor(eqv, eqv, ltg, ALU.mult))
                link(nc.vector.tensor_tensor(cmp_, cmp_, eqv, ALU.add))
                link(nc.vector.tensor_reduce(rank, cmp_.rearrange("p (i g) -> p i g", g=NG), AX.X, ALU.add))
                link(nc.vector.tensor_scalar(gmask, rank, 3.5, None, ALU.is_lt))
                gm = gmask.rearrange("p (t g) -> p t g", t=NT).unsqueeze(3).broadcast_to([P, NT, NG, GS])
                link(nc.vector.tensor_tensor(v4(sel), v4(sel), gm, ALU.mult))
                link(nc.vector.tensor_scalar(gmask, gmask, -1.0, 1e30, ALU.add, ALU.mult))
                link(nc.vector.tensor_tensor(v4(sel), v4(sel), gm, ALU.add))
                for t in range(NT):
                    link(nc.vector.max(t8[:, t * 8:(t + 1) * 8], sel[:, t * NE:(t + 1) * NE]))
                    link(nc.vector.match_replace(rep[:, t * NE:(t + 1) * NE], t8[:, t * 8:(t + 1) * 8],
                                                 sel[:, t * NE:(t + 1) * NE], -3e30))
                link(nc.vector.tensor_scalar(rep, rep, -2e30, None, ALU.is_lt))
                link(nc.vector.tensor_tensor(G, sc, rep, ALU.mult))
                G3 = G.rearrange("p (t e) -> p t e", t=NT)
                link(nc.vector.tensor_reduce(den, G3, AX.X, ALU.add))
                link(nc.vector.reciprocal(den, den))
                link(nc.vector.tensor_scalar(den, den, ROUTED_SCALE, None, ALU.mult))
                link(nc.vector.tensor_tensor(G3, G3, den.unsqueeze(2).broadcast_to([P, NT, NE]), ALU.mult))
                v.wait_ge(e_h, 16)
                for t in range(NT):
                    link(nc.vector.tensor_scalar(acc[:, t, :], acc[:, t, :], ALPHA, None, ALU.mult))

        top[0] = after_G
        gu = [carve(KD * 2 * FF).rearrange("p (k n) -> p k n", k=KD) for _ in range(2)]
        dn = [carve(2 * D).rearrange("p (f n) -> p f n", f=2) for _ in range(2)]
        hid = carve(2 * SEQ).rearrange("p (f s) -> p f s", f=2)
        sl = [carve(HALF) for _ in range(2)]
        x_w = [sem("x_w0"), sem("x_w1")]
        x_read, x_gu, x_sl, x_hid, x_dn, x_acc = (sem("x_" + n) for n in ("read", "gu", "sl", "hid", "dn", "acc"))
        gu_v = a["exp_w_gu"].rearrange("e (k p) n -> e p k n", p=P)
        dn_v = a["exp_w_down"].rearrange("e (f p) n -> e p f n", p=P)
        with nc.Block() as block:
            @block.sync
            def _(sp):
                with sp.Fori(0, NE // 2) as i:
                    for u in range(2):
                        e = 2 * i + u
                        sp.wait_ge(x_read, e + 1)
                        sp.dma_start(gu[u], gu_v[bass.ds(e, 1)].rearrange("a p k n -> p (a k) n")).then_inc(x_w[u], 16)
                        sp.dma_start(dn[u], dn_v[bass.ds(e, 1)].rearrange("a p f n -> p (a f) n")).then_inc(x_w[u], 16)

            @block.tensor
            def _(pe):
                pe.sem_inc(x_read, 2)
                with pe.Fori(0, NE // 2) as i:
                    for u in range(2):
                        pe.wait_ge(x_w[u], 32 * i + 32)
                        for half in range(2):
                            hs = slice(half * HALF, (half + 1) * HALF)
                            for f in range(2):
                                q = 2 * half + f
                                pe.wait_ge(x_hid, 8 * i + 4 * u + q + 1)
                                for part in range(2):
                                    for k in range(KD):
                                        last = nc.tensor.matmul(PS[:, 2 * (q % 2) + part, :],
                                                                gu[u][:, k, part * FF + f * P:part * FF + (f + 1) * P],
                                                                hT[:, k, hs], start=(k == 0), stop=(k == KD - 1))
                                last.then_inc(x_gu, 1)
                        for t in range(NT):
                            if t % 4 == 0:
                                pe.wait_ge(x_hid, 8 * i + 4 * u + t // 2 + 4)
                            for j in range(2):
                                q = 2 * t + j
                                pe.wait_ge(x_acc, 32 * i + 16 * u + q + 1)
                                for f in range(2):
                                    last = nc.tensor.matmul(PS[:, 4 + q % 4, :], hid[:, f, t * P:(t + 1) * P],
                                                            dn[u][:, f, j * HALF:(j + 1) * HALF], start=(f == 0), stop=(f == 1))
                                last.then_inc(x_dn, 1)
                        pe.wait_ge(x_dn, 32 * i + 16 * (u + 1))
                        pe.sem_inc(x_read, 1)

            @block.scalar
            def _(act):
                with act.Fori(0, NE // 2) as i:
                    for u in range(2):
                        for q in range(4):
                            act.wait_ge(x_gu, 8 * i + 4 * u + q + 1)
                            act.wait_ge(x_hid, 8 * i + 4 * u + q + 1)
                            nc.scalar.activation(sl[q % 2], PS[:, 2 * (q % 2), :], ACT.Silu).then_inc(x_sl, 1)

            @block.vector
            def _(v):
                v.sem_inc(x_hid, 2)
                v.sem_inc(x_acc, 4)
                with v.Fori(0, NE // 2) as i:
                    for u in range(2):
                        for q in range(4):
                            half, f = q // 2, q % 2
                            v.wait_ge(x_sl, 8 * i + 4 * u + q + 1)
                            nc.vector.tensor_tensor(hid[:, f, half * HALF:(half + 1) * HALF], sl[q % 2],
                                                    PS[:, 2 * (q % 2) + 1, :], ALU.mult).then_inc(x_hid, 1)
                        for t in range(NT):
                            gate = G[:, bass.ds(2 * i + (t * NE + u), 1)]
                            for j in range(2):
                                q = 2 * t + j
                                v.wait_ge(x_dn, 32 * i + 16 * u + q + 1)
                                dst = acc[:, t, j * HALF:(j + 1) * HALF]
                                nc.vector.scalar_tensor_tensor(dst, PS[:, 4 + q % 4, :], gate, dst,
                                                               ALU.mult, ALU.add).then_inc(x_acc, 1)

        top[0] = after_acc
        gu = carve(KD * 2 * FF).rearrange("p (k n) -> p k n", k=KD)
        dn = carve(2 * D).rearrange("p (f n) -> p f n", f=2)
        hid = carve(2 * SEQ).rearrange("p (f s) -> p f s", f=2)
        sl = [carve(HALF) for _ in range(2)]
        wg = carve(KD * D).rearrange("p (k n) -> p k n", k=KD)
        we = carve(2 * D).rearrange("p (f n) -> p f n", f=2)
        pt = carve(NT * PLE).rearrange("p (t n) -> p t n", t=NT)
        pT = carve(2 * SEQ).rearrange("p (f s) -> p f s", f=2)
        bg_row, g_row, b_row = carve(D), carve(D), carve(D)
        pg = [carve(HALF) for _ in range(2)]
        st = carve(NT * 12).rearrange("p (t j s) -> p t j s", t=NT, j=2)
        mv = carve(NT * 2).rearrange("p (t s) -> p t s", t=NT)
        rstd = carve(NT)
        f_w, f_wg, f_p, f_par = sem("f_w"), sem("f_wg"), sem("f_p"), sem("f_par")
        (f_gu, f_sl, f_hid, f_dn, f_acc, f_tp, f_pT, f_pl, f_lg, f_sg, f_pr, f_chain, f_stat, f_rstd, f_out, f_st) = (
            sem("f_" + n) for n in ("gu", "sl", "hid", "dn", "acc", "tp", "pT", "pl", "lg", "sg", "pr", "chain", "stat",
                                    "rstd", "out", "st"))
        with nc.Block() as block:
            @block.sync
            def _(sp):
                sp.dma_start(gu, a["sh_w_gu"].rearrange("(k p) n -> p k n", p=P)).then_inc(f_w, 16)
                sp.dma_start(dn, a["sh_w_down"].rearrange("(f p) n -> p f n", p=P)).then_inc(f_w, 16)
                sp.dma_start(pt, a["p"].rearrange("(t p) n -> p t n", p=P)).then_inc(f_p, 16)
                sp.dma_start(wg, a["ple_w_g"].rearrange("(k p) n -> p k n", p=P)).then_inc(f_wg, 16)
                sp.dma_start(we, a["ple_w_e"].rearrange("(f p) n -> p f n", p=P)).then_inc(f_wg, 16)
                sp.dma_start(bg_row, row("ple_b_g", 0, D)).then_inc(f_par, 16)
                sp.dma_start(g_row, row("ln2_g", 0, D)).then_inc(f_par, 16)
                sp.dma_start(b_row, row("ln2_b", 0, D)).then_inc(f_par, 16)
                ov = out[0].rearrange("(t p) d -> t p d", p=P)
                for t in range(NT):
                    sp.wait_ge(f_out, t + 1)
                    sp.dma_start(ov[t], acc[:, t, :]).then_inc(f_st, 16)
                sp.wait_ge(f_st, 16 * NT)

            @block.tensor
            def _(pe):
                pe.wait_ge(f_w, 32)
                for q in range(4):
                    half, f = q // 2, q % 2
                    if q >= 2:
                        pe.wait_ge(f_hid, q - 1)
                    for part in range(2):
                        for k in range(KD):
                            last = nc.tensor.matmul(PS[:, 2 * (q % 2) + part, :],
                                                    gu[:, k, part * FF + f * P:part * FF + (f + 1) * P],
                                                    hT[:, k, half * HALF:(half + 1) * HALF], start=(k == 0), stop=(k == KD - 1))
                    last.then_inc(f_gu, 1)
                pe.wait_ge(f_p, 16)
                for t in range(0, NT, 2):
                    if t >= 4:
                        pe.wait_ge(f_pT, t // 2 - 1)
                    for c in range(4):
                        tt, f = t + c // 2, c % 2
                        last = nc.tensor.transpose(PS[:, 4 + (t // 2) % 2, c * P:(c + 1) * P], pt[:, tt, f * P:(f + 1) * P], ident)
                    last.then_inc(f_tp, 1)
                pe.wait_ge(f_hid, 4)
                for q in range(2 * NT):
                    t, j = q // 2, q % 2
                    if q >= 2:
                        pe.wait_ge(f_acc, q - 1)
                    for f in range(2):
                        last = nc.tensor.matmul(PS[:, 6 + q % 2, :], hid[:, f, t * P:(t + 1) * P],
                                                dn[:, f, j * HALF:(j + 1) * HALF], start=(f == 0), stop=(f == 1))
                    last.then_inc(f_dn, 1)
                pe.wait_ge(f_wg, 32)
                pe.wait_ge(f_pT, 4)
                for q in range(2 * NT):
                    t, j = q // 2, q % 2
                    js = slice(j * HALF, (j + 1) * HALF)
                    if q >= 2:
                        pe.wait_ge(f_pr, q - 1)
                    for k in range(KD):
                        last = nc.tensor.matmul(PS[:, q % 2, :], hT[:, k, t * P:(t + 1) * P], wg[:, k, js],
                                                start=(k == 0), stop=(k == KD - 1))
                    last.then_inc(f_pl, 1)
                    for f in range(2):
                        last = nc.tensor.matmul(PS[:, 2 + q % 2, :], pT[:, f, t * P:(t + 1) * P], we[:, f, js],
                                                start=(f == 0), stop=(f == 1))
                    last.then_inc(f_pl, 1)

            @block.scalar
            def _(act):
                for q in range(4):
                    act.wait_ge(f_gu, q + 1)
                    if q >= 2:
                        act.wait_ge(f_hid, q - 1)
                    nc.scalar.activation(sl[q % 2], PS[:, 2 * (q % 2), :], ACT.Silu).then_inc(f_sl, 1)
                for i in range(NT // 2):
                    act.wait_ge(f_tp, i + 1)
                    nc.scalar.activation(pT[:, :, 2 * i * P:(2 * i + 2) * P].rearrange("p f (t s) -> p t f s", t=2),
                                         PS[:, 4 + i % 2, :].rearrange("p (t f s) -> p t f s", t=2, f=2),
                                         ACT.Copy).then_inc(f_pT, 1)
                for q in range(2 * NT):
                    act.wait_ge(f_lg, q + 1)
                    nc.scalar.activation(pg[q % 2], pg[q % 2], ACT.Sigmoid).then_inc(f_sg, 1)

            @block.vector
            def _(v):
                link = chained(v, f_chain)
                for q in range(4):
                    half, f = q // 2, q % 2
                    v.wait_ge(f_sl, q + 1)
                    nc.vector.tensor_tensor(hid[:, f, half * HALF:(half + 1) * HALF], sl[q % 2], PS[:, 2 * (q % 2) + 1, :],
                                            ALU.mult).then_inc(f_hid, 1)
                for q in range(2 * NT):
                    t, j = q // 2, q % 2
                    v.wait_ge(f_dn, q + 1)
                    dst = acc[:, t, j * HALF:(j + 1) * HALF]
                    nc.vector.tensor_tensor(dst, dst, PS[:, 6 + q % 2, :], ALU.add).then_inc(f_acc, 1)
                v.wait_ge(f_par, 48)
                v.wait_ge(f_acc, 2 * NT)

                def logits(q):
                    j = q % 2
                    v.wait_ge(f_pl, 2 * q + 1)
                    if q >= 2:
                        v.wait_ge(f_pr, q - 1)
                    nc.vector.tensor_tensor(pg[q % 2], PS[:, q % 2, :], bg_row[:, j * HALF:(j + 1) * HALF],
                                            ALU.add).then_inc(f_lg, 1)

                logits(0)
                for q in range(2 * NT):
                    t, j = q // 2, q % 2
                    v.wait_ge(f_pl, 2 * q + 2)
                    v.wait_ge(f_sg, q + 1)
                    link(nc.vector.tensor_tensor(pg[q % 2], pg[q % 2], PS[:, 2 + q % 2, :], ALU.mult))
                    dst = acc[:, t, j * HALF:(j + 1) * HALF]
                    nc.vector.tensor_tensor(dst, dst, pg[q % 2], ALU.add).then_inc(f_pr, 1)
                    if q + 1 < 2 * NT:
                        logits(q + 1)
                    if j:
                        v.wait_ge(f_pr, q + 1)
                        ln_stats(v, link, acc, st, mv, t).then_inc(f_stat, 1)
                v.wait_ge(f_rstd, 2)
                for t in range(NT):
                    ln_apply(link, acc, t, mv, rstd, g_row, b_row).then_inc(f_out, 1)

            @block.gpsimd
            def _(pool):
                pool.wait_ge(f_stat, NT)
                nc.gpsimd.tensor_scalar(rstd, mv[:, :, 1], LN_EPS, None, ALU.add).then_inc(f_rstd, 1)
                pool.wait_ge(f_rstd, 1)
                nc.gpsimd.tensor_tensor(rstd, rstd, nhalf[:, 0:NT], ALU.pow).then_inc(f_rstd, 1)


def lay_out(inputs):
    f = {n: np.ascontiguousarray(np.asarray(x)) for n, x in inputs.items()}
    one = {n: (x if n in ("x", "p", "ln_in_g", "ln_in_b") else x[0]) for n, x in f.items()}
    one["p"] = f["p"][0, 0]
    cols = np.zeros((P, N_COLS), np.float32)

    def put(name, v):
        at, n = COLS[name]
        cols[:, at:at + n] = np.reshape(v, (n, P)).T

    b = one["b_in"]
    put("b_rg", b[C_RG:C_RG + W])
    put("b_qkv", b[C_QKV:C_QKV + 3 * W])
    put("b_gg", b[C_GG:C_GG + W])
    put("b_lx", b[C_LX:C_LX + W])
    put("b_lg", b[C_LG:C_LG + W])
    put("b_mg", b[C_MG:C_MG + 3 * D])
    put("ret_g", one["ret_norm_g"])
    put("ret_b", one["ret_norm_b"])
    put("gdn_w", one["gdn_conv_w"])
    put("gdn_g", one["gdn_norm_g"])
    put("lru_w", one["lru_conv_w"])
    put("lru_cb", one["lru_conv_b"])
    put("lru_br", one["lru_b_r"])
    put("lru_bi", one["lru_b_i"])
    put("lru_lam", one["lru_lambda"])
    one["cols"] = cols
    one["consts"] = constant_table()
    before = np.broadcast_to(np.arange(NG)[None, :] < np.arange(NG)[:, None], (NT, NG, NG))
    one["before"] = before.reshape(-1).astype(np.float32)
    for n in ("ret_norm_g", "ret_norm_b", "gdn_conv_w", "gdn_norm_g", "lru_conv_w", "lru_conv_b", "lru_b_r",
              "lru_b_i", "lru_lambda"):
        del one[n]
    return {n: np.ascontiguousarray(x) for n, x in one.items()}


def kernel(**inputs):
    import concourse.bacc as _bacc
    from concourse.bass_utils import run_bass_kernel_spmd as _run

    nc = _bacc.Bacc("TRN2", target_bir_lowering=False, num_devices=1)
    arrays = lay_out(inputs)
    a = {n: nc.dram_tensor(f"in_{n}", x.shape, F32, kind="ExternalInput").ap() for n, x in arrays.items()}
    out = nc.dram_tensor("out", (1, SEQ, D), F32, kind="ExternalOutput").ap()
    build(nc, a, out)
    r = _run(nc, [{f"in_{n}": x for n, x in arrays.items()}], core_ids=[0])
    return r.results[0]["out"]
```

```python
import math
from contextlib import ExitStack

import numpy as np

import concourse.bass as bass
from concourse import mybir

F32 = mybir.dt.float32
I32 = mybir.dt.int32
ALU = mybir.AluOpType
ACT = mybir.ActivationFunctionType
AX = mybir.AxisListType

P = 128
SEQ = 1024
D = 1024
NT = SEQ // P
KD = D // P
W = 512
H = 4
CH = W // P
HALF = 512
NE = 64
FF = 256
HX = D + NE
MAXB = NE + SEQ * 8 // P
TOPK = 8
NG = 8
GS = NE // NG
PLE = 256
LEVELS = 7
LN_EPS = 1e-5
ALPHA = 2.0 ** 0.25
LRU_C = 8.0
ROUTED_SCALE = 2.5

C_RQ, C_RK, C_RV, C_RG = 0, W, 2 * W, 3 * W
C_QKV = 4 * W
C_GG = C_QKV + 3 * W
C_BA = C_GG + W
C_LX = C_BA + 2 * H
C_LG = C_LX + W
C_MG = C_LG + W

COLS = {}


def _col_plan():
    at = 0
    for name, n in (("b_rg", 4), ("b_qkv", 12), ("b_gg", 4), ("b_lx", 4), ("b_lg", 4), ("b_mg", 24),
                    ("ret_g", 4), ("ret_b", 4), ("gdn_w", 48), ("gdn_g", 1), ("lru_w", 16), ("lru_cb", 4),
                    ("lru_br", 4), ("lru_bi", 4), ("lru_lam", 4)):
        COLS[name] = (at, n)
        at += n
    return at


N_COLS = _col_plan()

CONSTS = {}


def _const_plan():
    at = 0
    for name, n in (("ident", P), ("upper", P), ("level", LEVELS * P), ("rmask", H * P), ("rqdec", H * P),
                    ("rkdec", H), ("cos", NT * 64), ("sin", NT * 64)):
        CONSTS[name] = (at, n)
        at += n
    return at


N_CONSTS = _const_plan()
GAMMA = [1.0 - 2.0 ** (-5 - h) for h in range(H)]


def constant_table():
    out = np.zeros((P, N_CONSTS), np.float32)

    def put(name, a):
        at, n = CONSTS[name]
        out[:, at:at + n] = np.asarray(a, np.float32).reshape(P, n)

    i = np.arange(P)
    row, col = i[:, None], i[None, :]
    put("ident", np.eye(P))
    put("upper", row <= col)
    level = np.zeros((P, LEVELS, P))
    for s in range(LEVELS):
        b = 1 << s
        level[:, s, :] = (row // (2 * b) == col // (2 * b)) & ((col // b) % 2 == 1) & ((row // b) % 2 == 0)
    put("level", level)
    scale = float(P) ** -0.5
    lg = np.log1p(-np.exp2(-5.0 - np.arange(H)))
    diff = col - row
    rmask = np.zeros((P, H, P))
    qdec = np.zeros((P, H, P))
    for h in range(H):
        rmask[:, h, :] = np.where(diff >= 0, np.exp(lg[h] * np.maximum(diff, 0)), 0.0) * scale
        qdec[:, h, :] = np.exp(lg[h] * (col + 1.0))
    put("rmask", rmask)
    put("rqdec", qdec)
    put("rkdec", np.exp(lg[None, :] * (P - 1.0 - row)) * scale)
    inv = np.float32(10000.0) ** (-np.linspace(0.0, 1.0, 64, dtype=np.float32))
    ang = np.arange(SEQ, dtype=np.float32)[:, None] * inv[None, :].astype(np.float32)
    put("cos", np.cos(ang.astype(np.float32)).reshape(NT, P, 64).transpose(1, 0, 2))
    put("sin", np.sin(ang.astype(np.float32)).reshape(NT, P, 64).transpose(1, 0, 2))
    return out


def chained(eng, sem, start=0):
    n = [start]

    def link(ins):
        n[0] += 1
        ins.then_inc(sem, 1)
        eng.wait_ge(sem, n[0])
    return link


ARENA = 53000


def build(nc, a, out):
    ctx = ExitStack()
    with ctx:
        stage_sems = []

        def sem(name):
            stage_sems.append(nc.alloc_semaphore(name=name))
            return stage_sems[-1]

        def end_stage():
            nc.all_engine_barrier()
            nc.clear_and_free_semaphores(list(stage_sems))
            stage_sems.clear()
            nc.all_engine_barrier()

        A = ctx.enter_context(nc.sbuf_tensor("arena", [P, ARENA], F32))
        PS = ctx.enter_context(nc.psum_tensor("banks", [P, 8, 512], F32))
        h_d = nc.dram_tensor("h_scratch", (P, NT, D), F32).ap()
        hx_d = nc.dram_tensor("hx_scratch", (SEQ + P, HX), F32).ap()
        acc_d = nc.dram_tensor("acc_scratch", (SEQ + P, D), F32).ap()
        slot_d = nc.dram_tensor("slot_scratch", (MAXB * P, 1), F32).ap()
        y_d = {n: nc.dram_tensor(f"y_{n}_scratch", (P, CH, SEQ), F32).ap() for n in ("ret", "lru")}

        top = [0]

        def carve(n, at=None):
            at0 = top[0] if at is None else at
            if at is None:
                top[0] += n
            assert at0 + n <= ARENA, (at0, n)
            return A[:, at0:at0 + n]

        cst = carve(N_CONSTS)
        cols = carve(N_COLS)

        def const(name):
            at, n = CONSTS[name]
            return cst[:, at:at + n]

        def col(name, i, n=1):
            at, _ = COLS[name]
            return cols[:, at + i:at + i + n]

        ident = const("ident")
        nhalf = carve(64)
        upper = const("upper")
        hT = carve(KD * SEQ).rearrange("p (k s) -> p k s", k=KD)
        base = top[0]

        def region():
            top[0] = base

        r_w = [nc.alloc_semaphore(name=f"r_w{i}") for i in range(2)]
        r_par = nc.alloc_semaphore(name="r_par")
        g_w = [nc.alloc_semaphore(name=f"g_w{i}") for i in range(2)]
        o_w = [nc.alloc_semaphore(name=f"o_w{i}") for i in range(2)]
        h_saved = nc.alloc_semaphore(name="h_saved")
        ret_saved = nc.alloc_semaphore(name="ret_saved")
        R_RING = base + 3 * NT * W + CH * SEQ
        PADS = SEQ + 4
        G_RING = base + 3 * CH * PADS + 2 * NT * W
        G_Y = G_RING + 2 * KD * W
        L_RAW = ARENA - CH * PADS - CH * SEQ
        L_YL = ARENA - CH * SEQ
        O_W = ARENA - KD * D
        r_ring = [carve(KD * W, R_RING + i * KD * W).rearrange("p (k n) -> p k n", k=KD) for i in range(2)]
        bias3 = carve(3 * W, R_RING + 2 * KD * W)
        g_ring = [carve(KD * W, G_RING + i * KD * W).rearrange("p (k n) -> p k n", k=KD) for i in range(2)]
        raw_l = carve(CH * PADS, L_RAW).rearrange("p (c s) -> p c s", c=CH)
        yl = carve(CH * SEQ, L_YL).rearrange("p (c s) -> p c s", c=CH)
        wo = carve(KD * D, O_W).rearrange("p (k n) -> p k n", k=KD)
        R_GROUPS = (C_RQ, C_RK, C_RV, C_RG, C_LX, C_LG)
        G_GROUPS = (C_QKV, C_QKV + W, C_QKV + 2 * W, C_GG)

        def tok3(ap):
            return ap.rearrange("p (t c) -> p t c", t=NT)

        def row(name, lo, n):
            return a[name][lo:lo + n].rearrange("(a n) -> a n", a=1).broadcast_to([P, n])

        w_in = a["w_in"]

        def w_cols(lo, n):
            return w_in[:, lo:lo + n].rearrange("(k p) n -> p k n", p=P)

        def ln_stats(v, link, src, st, mv, t):
            for j in range(2):
                link(nc.vector.bn_stats(st[:, t, j, :], src[:, t, j * HALF:(j + 1) * HALF]))
            return nc.vector.bn_aggr(mv[:, t, :], st[:, t, :, :])

        def ln_apply(link, dst, t, mv, rstd, g_row, b_row):
            link(nc.vector.tensor_scalar(dst[:, t, :], dst[:, t, :], mv[:, t, 0:1], rstd[:, t:t + 1],
                                         ALU.subtract, ALU.mult))
            link(nc.vector.tensor_tensor(dst[:, t, :], dst[:, t, :], g_row, ALU.mult))
            return nc.vector.tensor_tensor(dst[:, t, :], dst[:, t, :], b_row, ALU.add)

        def rstd_tile(pool, rstd, mv, t, stat, done, done0):
            pool.wait_ge(stat, t + 1)
            nc.gpsimd.tensor_scalar(rstd[:, t:t + 1], mv[:, t, 1:2], LN_EPS, None, ALU.add).then_inc(done, 1)
            pool.wait_ge(done, done0 + 2 * t + 1)
            nc.gpsimd.tensor_tensor(rstd[:, t:t + 1], rstd[:, t:t + 1], nhalf[:, 0:1], ALU.pow).then_inc(done, 1)

        def transpose_tile(pe, src, t, ready, moved, freed):
            pe.wait_ge(ready, t + 1)
            for j in range(2):
                i = 2 * t + j
                if i >= 4:
                    pe.wait_ge(freed, i - 3)
                for c in range(4):
                    k = 4 * j + c
                    last = nc.tensor.transpose(PS[:, i % 4, c * P:(c + 1) * P], src[:, t, k * P:(k + 1) * P], ident)
                last.then_inc(moved, 1)

        def copy_transposed(act, dst, moved, freed):
            for i in range(2 * NT):
                t, j = i // 2, i % 2
                act.wait_ge(moved, i + 1)
                nc.scalar.activation(dst[:, 4 * j:4 * j + 4, t * P:(t + 1) * P],
                                     PS[:, i % 4, :].rearrange("p (c s) -> p c s", c=4), ACT.Copy).then_inc(freed, 1)

        region()
        h = tok3(carve(NT * D))
        g_row, b_row = carve(D), carve(D)
        st = carve(NT * 12).rearrange("p (t j s) -> p t j s", t=NT, j=2)
        mv = carve(NT * 2).rearrange("p (t s) -> p t s", t=NT)
        rstd = carve(NT)
        assert top[0] <= R_RING
        a_par, a_x, a_chain = sem("a_params"), [sem(f"a_x{i}") for i in range(4)], sem("a_chain")
        a_stat, a_rstd, a_h, a_tp, a_hT = (sem(n) for n in ("a_stat", "a_rstd", "a_h", "a_tp", "a_hT"))
        with nc.Block() as block:
            @block.sync
            def _(sp):
                xv = a["x"][0].rearrange("(t p) d -> p t d", p=P)
                for i in range(4):
                    sp.dma_start(h[:, 2 * i:2 * i + 2, :], xv[:, 2 * i:2 * i + 2, :]).then_inc(a_x[i], 16)
                for g in range(2):
                    sp.dma_start(r_ring[g], w_cols(R_GROUPS[g], W)).then_inc(r_w[g], 16)
                sp.dma_start(bias3, row("b_in", 0, 3 * W)).then_inc(r_par, 16)
                sp.wait_ge(a_h, NT)
                sp.dma_start(h_d, h).then_inc(h_saved, 16)

            @block.scalar
            def _(act):
                act.dma_start(cst, a["consts"]).then_inc(a_par, 16)
                act.dma_start(cols, a["cols"]).then_inc(a_par, 16)
                act.dma_start(g_row, row("ln_in_g", 0, D)).then_inc(a_par, 16)
                act.dma_start(b_row, row("ln_in_b", 0, D)).then_inc(a_par, 16)
                copy_transposed(act, hT, a_tp, a_hT)

            @block.vector
            def _(v):
                link = chained(v, a_chain)
                for t in range(NT):
                    v.wait_ge(a_x[t // 2], 16)
                    ln_stats(v, link, h, st, mv, t).then_inc(a_stat, 1)
                    if t == 1:
                        v.wait_ge(a_par, 64)
                    if t:
                        v.wait_ge(a_rstd, 2 * t + 1)
                        ln_apply(link, h, t - 1, mv, rstd, g_row, b_row).then_inc(a_h, 1)
                v.wait_ge(a_rstd, 2 * NT + 1)
                ln_apply(link, h, NT - 1, mv, rstd, g_row, b_row).then_inc(a_h, 1)

            @block.gpsimd
            def _(pool):
                nc.gpsimd.memset(nhalf, -0.5).then_inc(a_rstd, 1)
                pool.wait_ge(a_rstd, 1)
                for t in range(NT):
                    rstd_tile(pool, rstd, mv, t, a_stat, a_rstd, 1)

            @block.tensor
            def _(pe):
                pe.wait_ge(a_par, 64)
                for t in range(NT):
                    transpose_tile(pe, h, t, a_h, a_tp, a_hT)

        region()
        q3, k3, v3 = (tok3(carve(NT * W)) for _ in range(3))
        yr = carve(CH * SEQ).rearrange("p (c s) -> p c s", c=CH)
        ring = r_ring
        top[0] += 2 * KD * W + 3 * W
        qr, kr, kd, ta, tb = (carve(W) for _ in range(5))
        qTs, kTs, qTd, sT, on, yt = (carve(W) for _ in range(6))
        sq, cen = ta, tb
        S = [carve(W) for _ in range(2)]
        stat4 = carve(3 * H)
        assert top[0] <= L_RAW
        (r_grp, r_job, r_evD, r_evA, r_chain, r_rot, r_tq, r_tk, r_qT, r_kT, r_qTd, r_sc, r_sT, r_dS, r_S,
         r_o, r_var, r_rstd, r_on, r_to, r_yt, r_y) = (sem("r_" + n) for n in (
             "grp", "job", "evD", "evA", "chain", "rot", "tq", "tk", "qT", "kT", "qTd", "sc", "sT", "dS", "S",
             "o", "var", "rstd", "on", "to", "yt", "y"))

        def heads(ap):
            return ap.rearrange("p (h c) -> p h c", h=H)

        def per_head(ap4, n=P):
            return ap4.unsqueeze(2).broadcast_to([P, H, n])

        def project_tokens(pe, wt, bank, t):
            for k in range(KD):
                last = nc.tensor.matmul(PS[:, bank, :], hT[:, k, t * P:(t + 1) * P], wt[:, k, :],
                                        start=(k == 0), stop=(k == KD - 1))
            return last

        def project_channels(pe, wt, bank, ct, half):
            for k in range(KD):
                last = nc.tensor.matmul(PS[:, bank, :], wt[:, k, ct * P:(ct + 1) * P],
                                        hT[:, k, half * HALF:(half + 1) * HALF],
                                        start=(k == 0), stop=(k == KD - 1))
            return last

        with nc.Block() as block:
            @block.sync
            def _(sp):
                for g in range(2, 6):
                    sp.wait_ge(r_grp, g - 1)
                    sp.dma_start(ring[g % 2], w_cols(R_GROUPS[g], W)).then_inc(r_w[g % 2], 16)
                sp.wait_ge(r_y, NT)
                sp.dma_start(y_d["ret"], yr).then_inc(ret_saved, 16)

            @block.tensor
            def _(pe):
                def freed(job):
                    if job < 0:
                        return
                    if job < 24:
                        pe.wait_ge(r_evD, job + 1)
                    else:
                        pe.wait_ge(r_evA, job - 23)

                for g in range(4):
                    pe.wait_ge(r_w[g % 2], 16 * (g // 2 + 1))
                    for j in range(8):
                        job = 8 * g + j
                        freed(job - 2)
                        if g < 3:
                            last = project_tokens(pe, ring[g % 2], job % 2, j)
                        else:
                            last = project_channels(pe, ring[g % 2], job % 2, j // 2, j % 2)
                        last.then_inc(r_job, 1)
                    pe.wait_ge(r_job, 8 * (g + 1))
                    pe.sem_inc(r_grp, 1)

                def lru_quarter(t, quarter):
                    job = 32 + 2 * t + quarter // 2
                    g, j, k0 = job // 8, job % 8, quarter % 2 * CH
                    if k0 == 0:
                        if j == 0:
                            pe.wait_ge(r_w[g % 2], 16 * (g // 2 + 1))
                        freed(job - 2)
                    for k in range(k0, k0 + CH):
                        last = nc.tensor.matmul(PS[:, job % 2, :], ring[g % 2][:, k, (j // 2) * P:(j // 2 + 1) * P],
                                                hT[:, k, (j % 2) * HALF:(j % 2 + 1) * HALF],
                                                start=(k == 0), stop=(k == KD - 1))
                    if k0:
                        last.then_inc(r_job, 1)

                for t in range(NT):
                    pe.wait_ge(r_rot, t + 1)
                    if t:
                        pe.wait_ge(r_qT, t)
                        pe.wait_ge(r_kT, t)
                    for hh in range(H):
                        last = nc.tensor.transpose(PS[:, 2, hh * P:(hh + 1) * P], qr[:, hh * P:(hh + 1) * P], ident)
                    last.then_inc(r_tq, 1)
                    for hh in range(H):
                        last = nc.tensor.transpose(PS[:, 3, hh * P:(hh + 1) * P], kr[:, hh * P:(hh + 1) * P], ident)
                    last.then_inc(r_tk, 1)
                    if t:
                        pe.wait_ge(r_S, t)
                    for hh in range(H):
                        hs = slice(hh * P, (hh + 1) * P)
                        last = nc.tensor.matmul(PS[:, 6, hs], kd[:, hs], v3[:, t, hs], start=True, stop=True)
                    last.then_inc(r_dS, 1)
                    lru_quarter(t, 0)
                    pe.wait_ge(r_qT, t + 1)
                    pe.wait_ge(r_kT, t + 1)
                    if t:
                        pe.wait_ge(r_sT, t)
                    for hh in range(H):
                        hs = slice(hh * P, (hh + 1) * P)
                        last = nc.tensor.matmul(PS[:, 4, hs], kTs[:, hs], qTs[:, hs], start=True, stop=True)
                    last.then_inc(r_sc, 1)
                    lru_quarter(t, 1)
                    pe.wait_ge(r_sT, t + 1)
                    if t:
                        pe.wait_ge(r_qTd, t + 1)
                        pe.wait_ge(r_S, t)
                        pe.wait_ge(r_on, t)
                    for hh in range(H):
                        hs = slice(hh * P, (hh + 1) * P)
                        last = nc.tensor.matmul(PS[:, 5, hs], sT[:, hs], v3[:, t, hs], start=True, stop=(t == 0))
                        if t:
                            last = nc.tensor.matmul(PS[:, 5, hs], qTd[:, hs], S[t % 2][:, hs], start=False, stop=True)
                    last.then_inc(r_o, 1)
                    lru_quarter(t, 2)
                    pe.wait_ge(r_on, t + 1)
                    if t:
                        pe.wait_ge(r_yt, t)
                    for hh in range(H):
                        hs = slice(hh * P, (hh + 1) * P)
                        last = nc.tensor.transpose(PS[:, 7, hs], on[:, hs], ident)
                    last.then_inc(r_to, 1)
                    lru_quarter(t, 3)

            @block.scalar
            def _(act):
                def lru_evacuate(job):
                    g, j = job // 8, job % 8
                    half = (j % 2) * HALF
                    act.wait_ge(r_job, job + 1)
                    if g == 4:
                        nc.scalar.activation(raw_l[:, j // 2, 3 + half:3 + half + HALF], PS[:, job % 2, :],
                                             ACT.Identity, bias=col("b_lx", j // 2)).then_inc(r_evA, 1)
                    else:
                        nc.scalar.activation(yl[:, j // 2, half:half + HALF], PS[:, job % 2, :],
                                             ACT.Gelu_apprx_tanh, bias=col("b_lg", j // 2)).then_inc(r_evA, 1)

                for j in range(8):
                    act.wait_ge(r_job, 24 + j + 1)
                    nc.scalar.activation(yr[:, j // 2, (j % 2) * HALF:(j % 2 + 1) * HALF], PS[:, j % 2, :], ACT.Silu,
                                         bias=col("b_rg", j // 2)).then_inc(r_evA, 1)
                for t in range(NT):
                    act.wait_ge(r_tq, t + 1)
                    if t:
                        act.wait_ge(r_sc, t)
                        act.wait_ge(r_qTd, t)
                    nc.scalar.activation(qTs, PS[:, 2, :], ACT.Copy).then_inc(r_qT, 1)
                    act.wait_ge(r_tk, t + 1)
                    nc.scalar.activation(kTs, PS[:, 3, :], ACT.Copy).then_inc(r_kT, 1)
                    lru_evacuate(32 + 2 * t)
                    act.wait_ge(r_to, t + 1)
                    if t:
                        act.wait_ge(r_y, t)
                    for hh in range(H):
                        hs = slice(hh * P, (hh + 1) * P)
                        last = nc.scalar.activation(yt[:, hs], PS[:, 7, hs], ACT.Identity,
                                                    bias=col("ret_b", hh), scale=col("ret_g", hh))
                    last.then_inc(r_yt, 1)
                    lru_evacuate(33 + 2 * t)

            @block.vector
            def _(v):
                link = chained(v, r_chain)
                v.wait_ge(r_par, 16)
                v.wait_ge(h_saved, 16)
                for job in range(24):
                    g, t = job // 8, job % 8
                    v.wait_ge(r_job, job + 1)
                    nc.vector.tensor_tensor((q3, k3, v3)[g][:, t, :], PS[:, job % 2, :],
                                            bias3[:, g * W:(g + 1) * W], ALU.add).then_inc(r_evD, 1)
                v.wait_ge(r_evD, 24)
                for t in range(NT):
                    cos_t = const("cos")[:, t * 64:(t + 1) * 64]
                    sin_t = const("sin")[:, t * 64:(t + 1) * 64]
                    if t:
                        v.wait_ge(r_tk, t)
                        v.wait_ge(r_dS, t)
                        v.wait_ge(r_on, t)
                    for src, dst in ((q3, qr), (k3, kr)):
                        x4 = src[:, t, :].rearrange("p (h f c) -> p h f c", h=H, f=2)
                        d4 = dst.rearrange("p (h f c) -> p h f c", h=H, f=2)
                        a4 = ta.rearrange("p (h f c) -> p h f c", h=H, f=2)
                        b4 = tb.rearrange("p (h f c) -> p h f c", h=H, f=2)
                        cb = cos_t.unsqueeze(1).broadcast_to([P, H, 64])
                        sb_ = sin_t.unsqueeze(1).broadcast_to([P, H, 64])
                        nc.vector.tensor_tensor(a4[:, :, 0, :], x4[:, :, 0, :], cb, ALU.mult)
                        nc.vector.tensor_tensor(a4[:, :, 1, :], x4[:, :, 1, :], cb, ALU.mult)
                        nc.vector.tensor_tensor(b4[:, :, 0, :], x4[:, :, 1, :], sb_, ALU.mult)
                        link(nc.vector.tensor_tensor(b4[:, :, 1, :], x4[:, :, 0, :], sb_, ALU.mult))
                        nc.vector.tensor_tensor(d4[:, :, 0, :], a4[:, :, 0, :], b4[:, :, 0, :], ALU.subtract)
                        link(nc.vector.tensor_tensor(d4[:, :, 1, :], a4[:, :, 1, :], b4[:, :, 1, :], ALU.add))
                    nc.vector.tensor_tensor(heads(kd), heads(kr), per_head(const("rkdec")), ALU.mult).then_inc(r_rot, 1)
                    v.wait_ge(r_qT, t + 1)
                    if t:
                        v.wait_ge(r_o, t)
                    nc.vector.tensor_tensor(qTd, qTs, const("rqdec"), ALU.mult).then_inc(r_qTd, 1)
                    v.wait_ge(r_sc, t + 1)
                    nc.vector.tensor_tensor(sT, PS[:, 4, :], const("rmask"), ALU.mult).then_inc(r_sT, 1)
                    v.wait_ge(r_dS, t + 1)
                    for hh in range(H):
                        hs = slice(hh * P, (hh + 1) * P)
                        if t == 0:
                            last = nc.vector.tensor_copy(S[1][:, hs], PS[:, 6, hs])
                        else:
                            last = nc.vector.scalar_tensor_tensor(S[(t + 1) % 2][:, hs], S[t % 2][:, hs],
                                                                  GAMMA[hh] ** P, PS[:, 6, hs], ALU.mult, ALU.add)
                    link(last)
                    last = nc.vector.memset(stat4[:, 0:1], 0.0)
                    last.then_inc(r_S, 1)
                    v.wait_ge(r_S, t + 1)
                    v.wait_ge(r_o, t + 1)
                    mean, var, rs = stat4[:, 0:H], stat4[:, H:2 * H], stat4[:, 2 * H:3 * H]
                    link(nc.vector.tensor_reduce(mean, heads(PS[:, 5, :]), AX.X, ALU.add))
                    link(nc.vector.tensor_scalar(mean, mean, 1.0 / P, None, ALU.mult))
                    link(nc.vector.tensor_tensor(heads(cen), heads(PS[:, 5, :]), per_head(mean), ALU.subtract))
                    link(nc.vector.tensor_tensor(sq, cen, cen, ALU.mult))
                    nc.vector.tensor_reduce(var, heads(sq), AX.X, ALU.add).then_inc(r_var, 1)
                    v.wait_ge(r_rstd, 2 * (t + 1))
                    if t:
                        v.wait_ge(r_to, t)
                    nc.vector.tensor_tensor(heads(on), heads(cen), per_head(rs), ALU.mult).then_inc(r_on, 1)

            @block.gpsimd
            def _(pool):
                var, rs = stat4[:, H:2 * H], stat4[:, 2 * H:3 * H]
                for t in range(NT):
                    pool.wait_ge(r_var, t + 1)
                    nc.gpsimd.tensor_scalar(rs, var, 1.0 / P, LN_EPS, ALU.mult, ALU.add).then_inc(r_rstd, 1)
                    pool.wait_ge(r_rstd, 2 * t + 1)
                    nc.gpsimd.tensor_tensor(rs, rs, nhalf[:, 0:H], ALU.pow).then_inc(r_rstd, 1)
                    pool.wait_ge(r_yt, t + 1)
                    pool.wait_ge(r_evA, 8)
                    ysl = yr[:, :, t * P:(t + 1) * P]
                    nc.gpsimd.tensor_tensor(ysl, heads(yt), ysl, ALU.mult).then_inc(r_y, 1)

        region()
        raw = raw_l
        xc = carve(CH * SEQ).rearrange("p (c s) -> p c s", c=CH)
        rg = carve(CH * SEQ).rearrange("p (c s) -> p c s", c=CH)
        ig = carve(CH * SEQ).rearrange("p (c s) -> p c s", c=CH)
        assert top[0] == R_RING - CH * SEQ
        top[0] = R_RING
        wri = carve(2 * CH * P).rearrange("p (g c n) -> p g c n", g=2, c=CH)
        th = [carve(SEQ) for _ in range(2)]
        sp_t = carve(8 * 32).rearrange("p (i n) -> p i n", i=8)
        lam8, nlam8 = carve(CH), carve(CH)
        assert top[0] <= G_RING and G_RING + 2 * KD * W <= L_RAW
        (l_par, l_chain, l_z, l_exp, l_lam, l_xc, l_gate, l_gev, l_mz, l_th, l_a, l_in, l_sq,
         l_y, l_st, l_pool) = (sem("l_" + n) for n in (
             "par", "chain", "z", "exp", "lam", "xc", "gate", "gev", "mz", "th", "a", "in", "sq",
             "y", "st", "pool"))

        def softplus_start(v, link, z, tmp, n, out_sem):
            link(nc.vector.tensor_scalar(tmp[:, 0, 0:n], z, -1.0, None, ALU.mult))
            nc.vector.tensor_tensor(tmp[:, 0, 0:n], tmp[:, 0, 0:n], z, ALU.min).then_inc(out_sem, 1)

        def softplus_end(link, z, tmp, n):
            e, w, w2, q = (tmp[:, i, 0:n] for i in (1, 2, 3, 4))
            link(nc.vector.tensor_scalar(w, e, 2.0, None, ALU.add))
            link(nc.vector.reciprocal(w, w))
            link(nc.vector.tensor_tensor(w, w, e, ALU.mult))
            link(nc.vector.tensor_tensor(w2, w, w, ALU.mult))
            link(nc.vector.tensor_scalar(q, w2, 1.0 / 17, None, ALU.mult))
            for c in (15, 13, 11, 9, 7, 5, 3):
                link(nc.vector.scalar_tensor_tensor(q, q, 1.0 / c, w2, ALU.add, ALU.mult))
            link(nc.vector.scalar_tensor_tensor(q, q, 1.0, w, ALU.add, ALU.mult))
            link(nc.vector.tensor_scalar(q, q, 2.0, None, ALU.mult))
            link(nc.vector.scalar_tensor_tensor(q, z, 0.0, q, ALU.max, ALU.add))
            return q

        with nc.Block() as block:
            @block.sync
            def _(sp):
                sp.wait_ge(l_mz, 1)
                for g, name in enumerate(("lru_w_r", "lru_w_i")):
                    wv = a[name].rearrange("(c b) i j -> b i c j", b=2)
                    for b in range(2):
                        sp.dma_start(wri[b * 64:(b + 1) * 64, g, :, b * 64:(b + 1) * 64], wv[b]).then_inc(l_par, 16)
                for g in range(2):
                    sp.dma_start(g_ring[g], w_cols(G_GROUPS[g], W)).then_inc(g_w[g], 16)
                sp.wait_ge(l_y, CH)
                sp.dma_start(y_d["lru"], yl).then_inc(l_st, 16)
                sp.wait_ge(l_st, 16)
                sp.wait_ge(ret_saved, 16)

            @block.tensor
            def _(pe):
                pe.wait_ge(l_par, 64)
                n = 0
                for c in range(CH):
                    pe.wait_ge(l_xc, c + 1)
                    for g in range(2):
                        for half in range(2):
                            if n >= 4:
                                pe.wait_ge(l_gev, n - 3)
                            nc.tensor.matmul(PS[:, 2 + n % 4, :], wri[:, g, c, :], xc[:, c, half * HALF:(half + 1) * HALF],
                                             start=True, stop=True).then_inc(l_gate, 1)
                            n += 1

            @block.scalar
            def _(act):
                act.wait_ge(l_z, 1)
                nc.scalar.activation(sp_t[:, 1, 0:CH], sp_t[:, 0, 0:CH], ACT.Exp).then_inc(l_exp, 1)
                n = 0
                for c in range(CH):
                    for g in range(2):
                        for half in range(2):
                            act.wait_ge(l_gate, n + 1)
                            nc.scalar.activation((rg, ig)[g][:, c, half * HALF:(half + 1) * HALF], PS[:, 2 + n % 4, :],
                                                 ACT.Sigmoid, bias=col(("lru_br", "lru_bi")[g], c)).then_inc(l_gev, 1)
                            n += 1
                act.wait_ge(l_gev, 16)
                act.wait_ge(l_lam, 1)
                for c in range(CH):
                    if c >= 2:
                        act.wait_ge(l_in, c - 1)
                    nc.scalar.activation(th[c % 2], rg[:, c, :], ACT.Tanh, scale=nlam8[:, c:c + 1]).then_inc(l_th, 1)
                    act.wait_ge(l_th, c + 1)
                    nc.scalar.activation(rg[:, c, :], rg[:, c, :], ACT.Exp, scale=lam8[:, c:c + 1]).then_inc(l_a, 1)
                for c in range(CH):
                    act.wait_ge(l_in, c + 1)
                    nc.scalar.activation(raw[:, c, 0:SEQ], raw[:, c, 0:SEQ], ACT.Sqrt).then_inc(l_sq, 1)

            @block.vector
            def _(v):
                link = chained(v, l_chain)
                lam = sp_t[:, 7, 0:CH]
                link(nc.vector.tensor_scalar(lam, col("lru_lam", 0, CH), -1.0, None, ALU.mult))
                softplus_start(v, link, lam, sp_t, CH, l_z)
                for g in range(2):
                    nc.vector.memset(wri[:, g, :, :], 0.0)
                for c in range(CH):
                    last = nc.vector.memset(raw[:, c, 0:3], 0.0)
                link(last)
                nc.vector.memset(sp_t[:, 6, 0:1], 0.0).then_inc(l_mz, 1)
                v.wait_ge(l_exp, 1)
                sp_lam = softplus_end(link, lam, sp_t, CH)
                link(nc.vector.tensor_scalar(lam8, sp_lam, -LRU_C, None, ALU.mult))
                nc.vector.tensor_scalar(nlam8, sp_lam, LRU_C, None, ALU.mult).then_inc(l_lam, 1)
                v.wait_ge(l_mz, 1)
                for c in range(CH):
                    tap = [col("lru_w", 4 * j + c) for j in range(4)]
                    link(nc.vector.tensor_scalar(xc[:, c, :], raw[:, c, 3:3 + SEQ], tap[3], col("lru_cb", c),
                                                 ALU.mult, ALU.add))
                    for j in range(3):
                        ins = nc.vector.scalar_tensor_tensor(xc[:, c, :], raw[:, c, j:j + SEQ], tap[j], xc[:, c, :],
                                                             ALU.mult, ALU.add)
                        if j < 2:
                            link(ins)
                    ins.then_inc(l_xc, 1)
                v.wait_ge(l_xc, CH)
                for c in range(CH):
                    v.wait_ge(l_a, c + 1)
                    link(nc.vector.tensor_tensor(raw[:, c, 0:SEQ], rg[:, c, :], rg[:, c, :], ALU.mult))
                    nc.vector.scalar_tensor_tensor(raw[:, c, 0:SEQ], raw[:, c, 0:SEQ], 1.0, th[c % 2],
                                                   ALU.add, ALU.mult).then_inc(l_in, 1)
                for c in range(CH):
                    v.wait_ge(l_sq, c + 1)
                    link(nc.vector.tensor_tensor(ig[:, c, :], ig[:, c, :], xc[:, c, :], ALU.mult))
                    link(nc.vector.tensor_tensor(ig[:, c, :], ig[:, c, :], raw[:, c, 0:SEQ], ALU.mult))
                    link(nc.vector.tensor_tensor_scan(xc[:, c, :], rg[:, c, :], ig[:, c, :], 0.0, ALU.mult, ALU.add))
                    nc.vector.tensor_tensor(yl[:, c, :], yl[:, c, :], xc[:, c, :], ALU.mult).then_inc(l_y, 1)

        region()
        QT = 3 * CH
        raw = carve(QT * PADS).rearrange("p (c s) -> p c s", c=QT)
        kn, vn = (carve(NT * W) for _ in range(2))
        assert top[0] == G_RING
        X, Xt, yg = (carve(NT * W) for _ in range(3))
        ring = g_ring
        kn, vn, X, Xt = (tok3(x) for x in (kn, vn, X, Xt))
        assert top[0] == G_Y + NT * W
        yg = yg.rearrange("p (c s) -> p c s", c=CH)
        mark = top[0]
        ctmp = [carve(SEQ) for _ in range(2)]
        top[0] = mark
        qk, sqk = carve(2 * W), carve(2 * W)
        qn, qd, kb, qT, kT, kbT, E = (carve(W) for _ in range(7))
        top2 = top[0]
        top[0] = mark
        Bt = [carve(W) for _ in range(2)]
        Pm = [carve(W) for _ in range(2)]
        kbg, vb, kd, nwT, vnew, sq, on = (carve(W) for _ in range(7))
        top[0] = max(top[0], top2)
        S = [carve(W) for _ in range(2)]
        ones = carve(P)
        wba = carve(KD * 2 * H).rearrange("p (k n) -> p k n", k=KD)
        gba = carve(NT * 2 * H).rearrange("p (t n) -> p t n", t=NT)
        small = carve(10 * 32).rearrange("p (i n) -> p i n", i=10)
        sp_t = carve(8 * 32).rearrange("p (i n) -> p i n", i=8)
        z, la, beta, gcC, gl, egc, egl, kdf, bg = (small[:, i, :] for i in range(9))
        rows8 = carve(8 + 3 * H)
        b_ba, b_dt, b_al, nea = rows8[:, 0:8], rows8[:, 8:12], rows8[:, 12:16], rows8[:, 16:20]
        rn, ss = carve(2 * H), carve(2 * H)
        (g_par, g_grp, g_job, g_ev, g_chain, g_cv, g_si, g_ba, g_bae, g_sm, g_act, g_cum, g_cume, g_fac, g_tqk, g_tv,
         g_cqk, g_cv3, g_ss, g_rn, g_prep, g_t4, g_c4, g_kk, g_gb, g_E, g_Ee, g_at, g_one) = (sem("g_" + n) for n in (
             "par", "grp", "job", "ev", "chain", "cv", "si", "ba", "bae", "sm", "act", "cum", "cume", "fac", "tqk", "tv",
             "cqk", "cv3", "ss", "rn", "prep", "t4", "c4", "kk", "gb", "E", "Ee", "at", "one"))
        (g_id, g_B, g_P, g_Pc, g_U, g_X, g_pre, g_wT, g_wTc, g_vn, g_vnc, g_o, g_dS, g_S, g_sq, g_var, g_rs, g_on, g_to,
         g_y) = (sem("g2_" + n) for n in (
             "id", "B", "P", "Pc", "U", "X", "pre", "wT", "wTc", "vn", "vnc", "o", "dS", "S", "sq", "var", "rs", "on", "to",
             "y"))

        def hd(ap, hh):
            return ap[:, hh * P:(hh + 1) * P]

        def tile4(ap, t):
            return ap[:, :, t * P:(t + 1) * P]

        def fac(f, t):
            return per_head(f[:, t * H:(t + 1) * H])

        with nc.Block() as block:
            @block.sync
            def _(sp):
                sp.dma_start(wba, w_in[:, C_BA:C_BA + 2 * H].rearrange("(k p) n -> p k n", p=P)).then_inc(g_par, 16)
                sp.dma_start(b_ba, row("b_in", C_BA, 2 * H)).then_inc(g_par, 16)
                sp.dma_start(b_dt, row("gdn_dt_bias", 0, H)).then_inc(g_par, 16)
                sp.dma_start(b_al, row("gdn_a_log", 0, H)).then_inc(g_par, 16)
                for g in range(2, 4):
                    sp.wait_ge(g_grp, g - 1)
                    sp.dma_start(ring[g % 2], w_cols(G_GROUPS[g], W)).then_inc(g_w[g % 2], 16)
                sp.wait_ge(g_y, NT)

            @block.tensor
            def _(pe):
                pe.wait_ge(g_par, 64)
                for t in range(NT):
                    for k in range(KD):
                        last = nc.tensor.matmul(PS[:, 2, t * 8:(t + 1) * 8], hT[:, k, t * P:(t + 1) * P], wba[:, k, :],
                                                start=(k == 0), stop=(k == KD - 1))
                last.then_inc(g_ba, 1)
                for g in range(4):
                    pe.wait_ge(g_w[g % 2], 16 * (g // 2 + 1))
                    for j in range(8):
                        job = 8 * g + j
                        if job >= 2:
                            pe.wait_ge(g_ev, job - 1)
                        project_channels(pe, ring[g % 2], job % 2, j // 2, j % 2).then_inc(g_job, 1)
                    pe.wait_ge(g_job, 8 * (g + 1))
                    pe.sem_inc(g_grp, 1)
                pe.wait_ge(g_sm, 1)
                pe.wait_ge(g_one, 1)
                nc.tensor.matmul(PS[:, 3, 0:32], upper, la, start=True, stop=True)
                nc.tensor.matmul(PS[:, 3, 32:64], ones, la, start=True, stop=True).then_inc(g_cum, 1)
                pe.wait_ge(g_fac, 1)
                pe.wait_ge(g_si, QT)
                pe.wait_ge(g_ev, 32)
                for t in range(NT):
                    if t:
                        pe.wait_ge(g_cqk, t)
                    for i in range(2 * H):
                        last = nc.tensor.transpose(PS[:, 2 + i // 4, (i % 4) * P:(i % 4 + 1) * P],
                                                   raw[:, i, t * P:(t + 1) * P], ident)
                    last.then_inc(g_tqk, 1)
                    if t:
                        pe.wait_ge(g_Ee, t)
                    for i in range(H):
                        last = nc.tensor.transpose(PS[:, 4, i * P:(i + 1) * P], raw[:, 8 + i, t * P:(t + 1) * P], ident)
                    last.then_inc(g_tv, 1)
                    pe.wait_ge(g_prep, t + 1)
                    if t:
                        pe.wait_ge(g_at, t)
                    for bank, src in ((5, qn), (6, qd), (0, kb)):
                        for hh in range(H):
                            last = nc.tensor.transpose(hd(PS[:, bank, :], hh), hd(src, hh), ident)
                    for hh in range(H):
                        last = nc.tensor.transpose(hd(PS[:, 7, :], hh), hd(kn[:, t, :], hh), ident)
                    last.then_inc(g_t4, 1)
                    pe.wait_ge(g_cv3, t + 1)
                    for hh in range(H):
                        last = nc.tensor.matmul(hd(PS[:, 4, :], hh), la[:, t * H + hh:t * H + hh + 1].broadcast_to([P, P]),
                                                upper, start=True, stop=True)
                    last.then_inc(g_gb, 1)
                    pe.wait_ge(g_c4, 4 * (t + 1))
                    for hh in range(H):
                        nc.tensor.matmul(hd(PS[:, 1, :], hh), hd(kT, hh), hd(kbT, hh), start=True, stop=True)
                    for hh in range(H):
                        last = nc.tensor.matmul(hd(PS[:, 5, :], hh), hd(kT, hh), hd(qT, hh), start=True, stop=True)
                    last.then_inc(g_kk, 1)
                n_i = LEVELS * NT

                def product(i):
                    t = i % NT
                    pe.wait_ge(g_B, i + 1)
                    if i >= 2:
                        pe.wait_ge(g_Pc, i - 1)
                    if i >= NT:
                        pe.wait_ge(g_X, i - NT + 1)
                    for hh in range(H):
                        last = nc.tensor.matmul(hd(PS[:, 2 + i % 2, :], hh), hd(Bt[i % 2], hh), hd(X[:, t, :], hh),
                                                start=True, stop=True)
                    last.then_inc(g_P, 1)

                def update(i):
                    t = i % NT
                    pe.wait_ge(g_Pc, i + 1)
                    if i >= 2:
                        pe.wait_ge(g_X, i - 1)
                    if i // NT < LEVELS - 1:
                        for hh in range(H):
                            nc.tensor.matmul(hd(PS[:, 4 + i % 2, :], hh), hd(Xt[:, t, :], hh), hd(Pm[i % 2], hh),
                                             start=True, stop=True)
                    for hh in range(H):
                        last = nc.tensor.matmul(hd(PS[:, 6 + i % 2, :], hh), hd(Pm[i % 2], hh), hd(Xt[:, t, :], hh),
                                                start=True, stop=True)
                    last.then_inc(g_U, 1)

                pe.wait_ge(g_at, NT)
                pe.wait_ge(g_id, 1)
                for i in range(n_i):
                    product(i)
                    if i:
                        update(i - 1)
                update(n_i - 1)
                pe.wait_ge(g_X, n_i)
                for t in range(NT):
                    pe.wait_ge(g_pre, t + 1)
                    if t:
                        pe.wait_ge(g_wTc, t)
                    for hh in range(H):
                        last = nc.tensor.matmul(hd(PS[:, 2, :], hh), hd(kbg, hh), hd(Xt[:, t, :], hh), start=True, stop=True)
                    last.then_inc(g_wT, 1)
                    if t:
                        pe.wait_ge(g_wTc, t + 1)
                        pe.wait_ge(g_S, t)
                        pe.wait_ge(g_vnc, t)
                    for hh in range(H):
                        last = nc.tensor.matmul(hd(PS[:, 3, :], hh), hd(Xt[:, t, :], hh), hd(vb, hh), start=True, stop=(t == 0))
                        if t:
                            last = nc.tensor.matmul(hd(PS[:, 3, :], hh), hd(nwT, hh), hd(S[t % 2], hh), start=False, stop=True)
                    last.then_inc(g_vn, 1)
                    pe.wait_ge(g_vnc, t + 1)
                    for hh in range(H):
                        last = nc.tensor.matmul(hd(PS[:, 5, :], hh), hd(kd, hh), hd(vnew, hh), start=True, stop=True)
                    last.then_inc(g_dS, 1)
                    if t:
                        pe.wait_ge(g_on, t)
                    for hh in range(H):
                        last = nc.tensor.matmul(hd(PS[:, 4, :], hh), raw[:, 8 + hh, t * P:(t + 1) * P], hd(vnew, hh),
                                                start=True, stop=(t == 0))
                        if t:
                            last = nc.tensor.matmul(hd(PS[:, 4, :], hh), raw[:, hh, t * P:(t + 1) * P], hd(S[t % 2], hh),
                                                    start=False, stop=True)
                    last.then_inc(g_o, 1)
                    pe.wait_ge(g_on, t + 1)
                    if t:
                        pe.wait_ge(g_y, t)
                    for hh in range(H):
                        last = nc.tensor.transpose(hd(PS[:, 6, :], hh), hd(on, hh), ident)
                    last.then_inc(g_to, 1)

            @block.scalar
            def _(act):
                def silu(c):
                    act.wait_ge(g_cv, c + 1)
                    nc.scalar.activation(raw[:, c, 0:SEQ], ctmp[c % 2], ACT.Silu).then_inc(g_si, 1)

                for job in range(32):
                    c, half = job // 2, job % 2
                    act.wait_ge(g_job, job + 1)
                    if job < 24:
                        nc.scalar.activation(raw[:, c, 3 + half * HALF:3 + (half + 1) * HALF], PS[:, job % 2, :],
                                             ACT.Identity, bias=col("b_qkv", c)).then_inc(g_ev, 1)
                    else:
                        nc.scalar.activation(yg[:, c - QT, half * HALF:(half + 1) * HALF], PS[:, job % 2, :],
                                             ACT.Silu, bias=col("b_gg", c - QT)).then_inc(g_ev, 1)
                    if half and 1 <= c <= QT:
                        silu(c - 1)
                act.wait_ge(g_bae, 1)
                nc.scalar.activation(beta.rearrange("p (t n) -> p t n", t=NT), gba[:, :, 0:H], ACT.Sigmoid).then_inc(g_act, 1)
                nc.scalar.activation(sp_t[:, 1, :], sp_t[:, 0, :], ACT.Exp).then_inc(g_act, 1)
                nc.scalar.activation(nea, b_al, ACT.Exp).then_inc(g_act, 1)
                act.wait_ge(g_cume, 1)
                nc.scalar.activation(egc, gcC, ACT.Exp).then_inc(g_act, 1)
                nc.scalar.activation(egl, gl, ACT.Exp).then_inc(g_act, 1)
                nc.scalar.activation(kdf, kdf, ACT.Exp).then_inc(g_act, 1)
                for t in range(NT):
                    act.wait_ge(g_tqk, t + 1)
                    if t:
                        act.wait_ge(g_prep, t)
                    nc.scalar.activation(qk.rearrange("p (b n) -> p b n", b=2), PS[:, 2:4, :], ACT.Copy).then_inc(g_cqk, 1)
                    act.wait_ge(g_tv, t + 1)
                    nc.scalar.activation(vn[:, t, :], PS[:, 4, :], ACT.Copy).then_inc(g_cv3, 1)
                    act.wait_ge(g_t4, t + 1)
                    if t:
                        act.wait_ge(g_kk, t)
                    nc.scalar.activation(qT, PS[:, 5, :], ACT.Copy).then_inc(g_c4, 1)
                    nc.scalar.activation(kT, PS[:, 7, :], ACT.Copy).then_inc(g_c4, 1)
                    nc.scalar.activation(kbT, PS[:, 0, :], ACT.Copy).then_inc(g_c4, 1)
                    nc.scalar.activation(tile4(raw[:, 0:4, :], t), heads(PS[:, 6, :]), ACT.Copy).then_inc(g_c4, 1)
                    act.wait_ge(g_E, t + 1)
                    nc.scalar.activation(E, E, ACT.Exp).then_inc(g_Ee, 1)
                for i in range(LEVELS * NT):
                    act.wait_ge(g_P, i + 1)
                    if i >= 2:
                        act.wait_ge(g_U, i - 1)
                    nc.scalar.activation(Pm[i % 2], PS[:, 2 + i % 2, :], ACT.Copy).then_inc(g_Pc, 1)
                for t in range(NT):
                    act.wait_ge(g_wT, t + 1)
                    if t:
                        act.wait_ge(g_vn, t)
                    nc.scalar.activation(nwT, PS[:, 2, :], ACT.Copy, scale=-1.0).then_inc(g_wTc, 1)
                    act.wait_ge(g_o, t + 1)
                    if t:
                        act.wait_ge(g_var, t)
                    nc.scalar.activation(sq, PS[:, 4, :], ACT.Square).then_inc(g_sq, 1)

            @block.vector
            def _(v):
                link = chained(v, g_chain)
                for c in range(QT):
                    nc.vector.memset(raw[:, c, 0:3], 0.0)
                nc.vector.memset(ones, 1.0).then_inc(g_one, 1)
                v.wait_ge(g_one, 1)
                v.wait_ge(g_ba, 1)
                v.wait_ge(g_par, 64)
                link(nc.vector.tensor_tensor(gba, PS[:, 2, 0:64].rearrange("p (t n) -> p t n", t=NT),
                                             b_ba.unsqueeze(1).broadcast_to([P, NT, 8]), ALU.add))
                link(nc.vector.tensor_tensor(z.rearrange("p (t n) -> p t n", t=NT), gba[:, :, H:2 * H],
                                             b_dt.unsqueeze(1).broadcast_to([P, NT, H]), ALU.add))
                softplus_start(v, link, z, sp_t, 32, g_bae)
                for c in range(QT):
                    v.wait_ge(g_ev, 2 * c + 2)
                    if c >= 2:
                        v.wait_ge(g_si, c - 1)
                    tap = [col("gdn_w", QT * j + c) for j in range(4)]
                    dst = ctmp[c % 2]
                    link(nc.vector.tensor_scalar(dst, raw[:, c, 3:3 + SEQ], tap[3], None, ALU.mult))
                    for j in range(3):
                        ins = nc.vector.scalar_tensor_tensor(dst, raw[:, c, j:j + SEQ], tap[j], dst, ALU.mult, ALU.add)
                        if j < 2:
                            link(ins)
                    ins.then_inc(g_cv, 1)
                v.wait_ge(g_act, 3)
                sp_z = softplus_end(link, z, sp_t, 32)
                link(nc.vector.tensor_scalar(nea, nea, -1.0, None, ALU.mult))
                nc.vector.tensor_tensor(la.rearrange("p (t n) -> p t n", t=NT), sp_z.rearrange("p (t n) -> p t n", t=NT),
                                        nea.unsqueeze(1).broadcast_to([P, NT, H]), ALU.mult).then_inc(g_sm, 1)
                v.wait_ge(g_cum, 1)
                link(nc.vector.tensor_copy(gcC, PS[:, 3, 0:32]))
                link(nc.vector.tensor_copy(gl, PS[:, 3, 32:64]))
                nc.vector.tensor_tensor(kdf, gl, gcC, ALU.subtract).then_inc(g_cume, 1)
                v.wait_ge(g_act, 6)
                nc.vector.tensor_tensor(bg, beta, egc, ALU.mult).then_inc(g_fac, 1)
                v.wait_ge(g_fac, 1)
                for t in range(NT):
                    v.wait_ge(g_cqk, t + 1)
                    link(nc.vector.tensor_tensor(sqk, qk, qk, ALU.mult))
                    nc.vector.tensor_reduce(ss, sqk.rearrange("p (h c) -> p h c", h=2 * H), AX.X, ALU.add).then_inc(g_ss, 1)
                    v.wait_ge(g_rn, 3 * (t + 1))
                    if t:
                        v.wait_ge(g_t4, t)
                    link(nc.vector.tensor_tensor(heads(qn), heads(qk[:, 0:W]), per_head(rn[:, 0:H]), ALU.mult))
                    link(nc.vector.tensor_tensor(heads(kn[:, t, :]), heads(qk[:, W:2 * W]), per_head(rn[:, H:2 * H]), ALU.mult))
                    link(nc.vector.tensor_tensor(heads(qd), heads(qn), fac(egc, t), ALU.mult))
                    nc.vector.tensor_tensor(heads(kb), heads(kn[:, t, :]), fac(beta, t), ALU.mult).then_inc(g_prep, 1)
                    v.wait_ge(g_gb, t + 1)
                    for hh in range(H):
                        last = nc.vector.tensor_scalar(hd(E, hh), hd(PS[:, 4, :], hh), gcC[:, t * H + hh:t * H + hh + 1], 0.0,
                                                       ALU.subtract, ALU.min)
                    last.then_inc(g_E, 1)
                    v.wait_ge(g_Ee, t + 1)
                    link(nc.vector.tensor_tensor(heads(E), heads(E), upper.unsqueeze(1).broadcast_to([P, H, P]), ALU.mult))
                    v.wait_ge(g_kk, t + 1)
                    nc.vector.tensor_tensor(tile4(raw[:, 4:8, :], t), heads(PS[:, 1, :]), heads(E), ALU.mult)
                    nc.vector.tensor_tensor(tile4(raw[:, 8:12, :], t), heads(PS[:, 5, :]), heads(E), ALU.mult).then_inc(g_at, 1)
                v.wait_ge(g_at, NT)
                v.wait_ge(g_kk, NT)
                eye4 = ident.unsqueeze(1).broadcast_to([P, H, P])
                for t in range(NT):
                    nc.vector.tensor_copy(heads(X[:, t, :]), eye4)
                    last = nc.vector.tensor_copy(heads(Xt[:, t, :]), eye4)
                last.then_inc(g_id, 1)
                v.wait_ge(g_id, 1)

                for i in range(LEVELS * NT):
                    s, t = i // NT, i % NT
                    v.wait_ge(g_U, i + 1)
                    if s < LEVELS - 1:
                        nc.vector.tensor_tensor(X[:, t, :], X[:, t, :], PS[:, 4 + i % 2, :], ALU.subtract)
                    nc.vector.tensor_tensor(Xt[:, t, :], Xt[:, t, :], PS[:, 6 + i % 2, :], ALU.subtract).then_inc(g_X, 1)
                for t in range(NT):
                    if t:
                        v.wait_ge(g_dS, t)
                        v.wait_ge(g_vn, t)
                    nc.vector.tensor_tensor(heads(kbg), heads(kn[:, t, :]), fac(bg, t), ALU.mult)
                    nc.vector.tensor_tensor(heads(vb), heads(vn[:, t, :]), fac(beta, t), ALU.mult)
                    nc.vector.tensor_tensor(heads(kd), heads(kn[:, t, :]), fac(kdf, t), ALU.mult).then_inc(g_pre, 1)
                    v.wait_ge(g_vn, t + 1)
                    if t:
                        v.wait_ge(g_o, t)
                    nc.vector.tensor_copy(vnew, PS[:, 3, :]).then_inc(g_vnc, 1)
                    v.wait_ge(g_dS, t + 1)
                    for hh in range(H):
                        if t == 0:
                            last = nc.vector.tensor_copy(hd(S[1], hh), hd(PS[:, 5, :], hh))
                        else:
                            last = nc.vector.scalar_tensor_tensor(hd(S[(t + 1) % 2], hh), hd(S[t % 2], hh),
                                                                  egl[:, t * H + hh:t * H + hh + 1], hd(PS[:, 5, :], hh),
                                                                  ALU.mult, ALU.add)
                    last.then_inc(g_S, 1)
                    v.wait_ge(g_S, t + 1)
                    v.wait_ge(g_sq, t + 1)
                    nc.vector.tensor_reduce(ss[:, 0:H], heads(sq), AX.X, ALU.add).then_inc(g_var, 1)
                    v.wait_ge(g_rs, 2 * (t + 1))
                    if t:
                        v.wait_ge(g_to, t)
                    nc.vector.tensor_tensor(heads(on), heads(PS[:, 4, :]), per_head(rn[:, 0:H]), ALU.mult).then_inc(g_on, 1)
                    v.wait_ge(g_to, t + 1)
                    nc.vector.scalar_tensor_tensor(tile4(yg, t), heads(PS[:, 6, :]), col("gdn_g", 0), tile4(yg, t),
                                                   ALU.mult, ALU.mult).then_inc(g_y, 1)

            @block.gpsimd
            def _(pool):
                for t in range(NT):
                    pool.wait_ge(g_ss, t + 1)
                    nc.gpsimd.tensor_scalar(rn, ss, 1e-6, None, ALU.add).then_inc(g_rn, 1)
                    pool.wait_ge(g_rn, 3 * t + 1)
                    nc.gpsimd.tensor_tensor(rn, rn, nhalf[:, 0:2 * H], ALU.pow).then_inc(g_rn, 1)
                    pool.wait_ge(g_rn, 3 * t + 2)
                    nc.gpsimd.tensor_scalar(rn[:, 0:H], rn[:, 0:H], float(P) ** -0.5, None, ALU.mult).then_inc(g_rn, 1)
                pool.wait_ge(g_at, NT)
                for i in range(LEVELS * NT):
                    s, t = i // NT, i % NT
                    if i >= 2:
                        pool.wait_ge(g_P, i - 1)
                    mask = const("level")[:, s * P:(s + 1) * P].unsqueeze(1).broadcast_to([P, H, P])
                    nc.gpsimd.tensor_tensor(heads(Bt[i % 2]), tile4(raw[:, 4:8, :], t), mask, ALU.mult).then_inc(g_B, 1)
                for t in range(NT):
                    pool.wait_ge(g_var, t + 1)
                    nc.gpsimd.tensor_scalar(rn[:, 0:H], ss[:, 0:H], 1.0 / P, 1e-6, ALU.mult, ALU.add).then_inc(g_rs, 1)
                    pool.wait_ge(g_rs, 2 * t + 1)
                    nc.gpsimd.tensor_tensor(rn[:, 0:H], rn[:, 0:H], nhalf[:, 0:H], ALU.pow).then_inc(g_rs, 1)

        region()
        mT = carve(KD * SEQ).rearrange("p (k s) -> p k s", k=KD)
        after_mT = top[0]
        ys = [carve(CH * SEQ).rearrange("p (c s) -> p c s", c=CH) for _ in range(2)]
        ys.insert(1, yg)
        wm = [carve(KD * 3 * P).rearrange("p (k n c) -> p k n c", k=KD, n=3) for _ in range(2)]
        wb = [carve(CH * 3 * P).rearrange("p (k n c) -> p k n c", k=CH, n=3) for _ in range(2)]
        sg = [carve(HALF) for _ in range(2)]
        prod = [carve(HALF) for _ in range(2)]
        assert top[0] <= G_Y and G_Y + CH * SEQ <= O_W
        m_y2 = sem("m_y_lru")
        m_y, m_w = sem("m_y_ret"), [sem("m_w0"), sem("m_w1")]
        m_read, m_g, m_b, m_sg, m_acc, m_chain = (sem("m_" + n) for n in ("read", "gate", "branch", "sg", "acc", "chain"))
        wmg_v = [w_in[:, C_MG + n * D:C_MG + (n + 1) * D].rearrange("(k p) c -> p k c", p=P) for n in range(3)]
        wbr_v = [a["w_branch"][n].rearrange("(k p) c -> p k c", p=P) for n in range(3)]
        PER = 6
        with nc.Block() as block:
            @block.sync
            def _(sp):
                with sp.Fori(0, KD // 2) as i:
                    for u in range(2):
                        dt = 2 * i + u
                        sp.wait_ge(m_read, dt + 1)
                        for n in range(3):
                            sp.dma_start(wm[u][:, :, n, :], wmg_v[n][:, :, bass.ds(dt * P, P)]).then_inc(m_w[u], 16)
                            sp.dma_start(wb[u][:, :, n, :], wbr_v[n][:, :, bass.ds(dt * P, P)]).then_inc(m_w[u], 16)
                wv = a["w_out"].rearrange("(k p) n -> p k n", p=P)
                for j in range(2):
                    sp.dma_start(wo[:, :, j * HALF:(j + 1) * HALF], wv[:, :, j * HALF:(j + 1) * HALF]).then_inc(o_w[j], 16)

            @block.tensor
            def _(pe):
                pe.sem_inc(m_read, 2)
                with pe.Fori(0, KD // 2) as i:
                    for u in range(2):
                        pe.wait_ge(m_w[u], 96 * i + 96)
                        for q in range(PER):
                            half, n = q // 3, q % 3
                            item = 12 * i + PER * u + q
                            b = 2 * ((PER * u + q) % 4)
                            hs = slice(half * HALF, (half + 1) * HALF)
                            pe.wait_ge(m_acc, item + 1)
                            for k in range(KD):
                                last = nc.tensor.matmul(PS[:, b, :], wm[u][:, k, n, :], hT[:, k, hs],
                                                        start=(k == 0), stop=(k == KD - 1))
                            last.then_inc(m_g, 1)
                            if n != 1:
                                pe.wait_ge((m_y, None, m_y2)[n], 16)
                            for k in range(CH):
                                last = nc.tensor.matmul(PS[:, b + 1, :], wb[u][:, k, n, :], ys[n][:, k, hs],
                                                        start=(k == 0), stop=(k == CH - 1))
                            last.then_inc(m_b, 1)
                        pe.wait_ge(m_b, 12 * i + PER * (u + 1))
                        pe.sem_inc(m_read, 1)

            @block.scalar
            def _(act):
                act.wait_ge(m_w[0], 96)
                act.dma_start(ys[0], y_d["ret"]).then_inc(m_y, 16)
                act.dma_start(ys[2], y_d["lru"]).then_inc(m_y2, 16)
                for item in range(KD * PER):
                    dt, n = item // PER, item % 3
                    act.wait_ge(m_g, item + 1)
                    act.wait_ge(m_acc, item + 3)
                    nc.scalar.activation(sg[item % 2], PS[:, 2 * (item % 4), :], ACT.Sigmoid,
                                         bias=col("b_mg", n * KD + dt)).then_inc(m_sg, 1)

            @block.vector
            def _(v):
                v.sem_inc(m_acc, 4)
                with v.Fori(0, KD // 2) as i:
                    for u in range(2):
                        for q in range(PER):
                            half, n = q // 3, q % 3
                            item = 12 * i + PER * u + q
                            b = 2 * ((PER * u + q) % 4) + 1
                            v.wait_ge(m_sg, item + 1)
                            v.wait_ge(m_b, item + 1)
                            dst = mT[:, bass.ds(2 * i + u, 1), half * HALF:(half + 1) * HALF].rearrange("p a s -> p (a s)")
                            if n == 0:
                                nc.vector.tensor_tensor(dst, PS[:, b, :], sg[q % 2], ALU.mult).then_inc(m_acc, 1)
                            else:
                                nc.vector.tensor_tensor(prod[q % 2], PS[:, b, :], sg[q % 2], ALU.mult).then_inc(m_chain, 1)
                                v.wait_ge(m_acc, item + 4)
                                v.wait_ge(m_chain, 8 * i + 4 * u + 2 * half + n)
                                nc.vector.tensor_tensor(dst, dst, prod[q % 2], ALU.add).then_inc(m_acc, 1)

        top[0] = after_mT
        h = tok3(carve(NT * D))
        g_row, b_row = carve(D), carve(D)
        st = carve(NT * 12).rearrange("p (t j s) -> p t j s", t=NT, j=2)
        mv = carve(NT * 2).rearrange("p (t s) -> p t s", t=NT)
        rstd = carve(NT)
        assert top[0] <= O_W
        o_par, o_h = sem("o_params"), sem("o_h")
        o_job, o_res, o_chain, o_stat, o_rstd, o_n, o_tp, o_hT, o_st = (sem("o_" + n) for n in (
            "job", "res", "chain", "stat", "rstd", "norm", "tp", "hT", "st"))
        with nc.Block() as block:
            @block.sync
            def _(sp):
                sp.dma_start(h, h_d).then_inc(o_h, 16)
                sp.dma_start(g_row, row("ln1_g", 0, D)).then_inc(o_par, 16)
                sp.dma_start(b_row, row("ln1_b", 0, D)).then_inc(o_par, 16)
                sp.wait_ge(o_n, NT)
                sp.dma_start(hx_d[0:SEQ, 0:D].rearrange("(t p) d -> p t d", p=P), h).then_inc(o_st, 16)
                sp.wait_ge(o_st, 16)

            @block.tensor
            def _(pe):
                pe.wait_ge(o_w[0], 16)
                pe.wait_ge(o_w[1], 16)
                for job in range(2 * NT):
                    t, j = job // 2, job % 2
                    if job >= 4:
                        pe.wait_ge(o_res, job - 3)
                    for k in range(KD):
                        last = nc.tensor.matmul(PS[:, 4 + job % 4, :], mT[:, k, t * P:(t + 1) * P],
                                                wo[:, k, j * HALF:(j + 1) * HALF], start=(k == 0), stop=(k == KD - 1))
                    last.then_inc(o_job, 1)
                    if j and t >= 2:
                        transpose_tile(pe, h, t - 2, o_n, o_tp, o_hT)
                transpose_tile(pe, h, NT - 2, o_n, o_tp, o_hT)
                transpose_tile(pe, h, NT - 1, o_n, o_tp, o_hT)

            @block.scalar
            def _(act):
                copy_transposed(act, hT, o_tp, o_hT)

            @block.vector
            def _(v):
                link = chained(v, o_chain)
                v.wait_ge(o_h, 16)
                v.wait_ge(o_par, 32)
                for job in range(2 * NT):
                    t, j = job // 2, job % 2
                    v.wait_ge(o_job, job + 1)
                    hs = h[:, t, j * HALF:(j + 1) * HALF]
                    nc.vector.scalar_tensor_tensor(hs, hs, ALPHA, PS[:, 4 + job % 4, :], ALU.mult, ALU.add).then_inc(o_res, 1)
                    if j:
                        v.wait_ge(o_res, job + 1)
                        ln_stats(v, link, h, st, mv, t).then_inc(o_stat, 1)
                        if t:
                            v.wait_ge(o_rstd, 2 * t)
                            ln_apply(link, h, t - 1, mv, rstd, g_row, b_row).then_inc(o_n, 1)
                v.wait_ge(o_rstd, 2 * NT)
                ln_apply(link, h, NT - 1, mv, rstd, g_row, b_row).then_inc(o_n, 1)

            @block.gpsimd
            def _(pool):
                for t in range(NT):
                    rstd_tile(pool, rstd, mv, t, o_stat, o_rstd, 0)

        end_stage()
        region()
        acc = tok3(carve(NT * D))
        pos_i = carve(NT * TOPK).bitcast(I32)
        bounds = carve(NE + 2).bitcast(I32)
        slot_i = carve(MAXB + 4).bitcast(I32)
        blk = carve(2 * (P + 2)).bitcast(I32)
        blk_e, blk_s = blk[:, 0:P + 1], blk[:, P + 2:2 * P + 3]
        pairs = carve(2).bitcast(I32)
        tok_id = carve(NT)
        pad_id = carve(P)
        after_acc = top[0]
        wr = carve(KD * NE).rearrange("p (k e) -> p k e", k=KD)
        rb = carve(NE)
        G = carve(NT * NE)
        after_G = top[0]
        sc, sel, rep = (carve(NT * NE) for _ in range(3))
        m8 = carve(NT * NG * 8)
        gsc, rank, gmask = (carve(NT * NG) for _ in range(3))
        cmp_, eqv, ltg = (carve(NT * NG * NG) for _ in range(3))
        t8 = carve(NT * 8)
        den = carve(NT)
        strict, ones = carve(P), carve(P)
        tot, off = (carve(NT * NE) for _ in range(2))
        cnt, nblk, bstart, one_e = (carve(NE) for _ in range(4))
        zero = carve(HX)
        alt, upto = carve(NE), carve(NE)
        e_col = carve(4)
        e_cols, e_rows = sem("e_cols"), sem("e_rows")
        e_tot = sem("e_totals")
        e_msk, e_pos, e_zero, e_st, e_slot = (sem("e_" + n) for n in ("mask", "pos", "zero", "store", "slots"))
        e_par, e_h, e_lg, e_sc, e_chain, e_cst, e_g, e_gd = (sem("e_" + n) for n in (
            "par", "h", "logits", "scores", "chain", "const", "gates", "gdram"))

        def v4(ap):
            return ap.rearrange("p (t g e) -> p t g e", t=NT, g=NG)

        with nc.Block() as block:
            @block.sync
            def _(sp):
                sp.dma_start(wr, a["router_w"].rearrange("(k p) e -> p k e", p=P)).then_inc(e_par, 16)
                sp.dma_start(rb, row("router_b", 0, NE)).then_inc(e_par, 16)
                sp.dma_start(ltg, a["before"].rearrange("(a n) -> a n", a=1).broadcast_to([P, NT * NG * NG])).then_inc(e_par, 16)
                sp.dma_start(tok_id, a["token_id"]).then_inc(e_par, 16)
                sp.dma_start(pad_id, a["pad_id"].rearrange("(a n) -> a n", a=1).broadcast_to([P, P])).then_inc(e_par, 16)
                sp.dma_start(acc, hx_d[0:SEQ, 0:D].rearrange("(t p) d -> p t d", p=P)).then_inc(e_h, 16)
                sp.wait_ge(e_par, 80)
                sp.dma_start(slot_d.rearrange("(b p) a -> b (p a)", p=P)[0:P, :], pad_id).then_inc(e_slot, 16)
                sp.wait_ge(e_zero, 1)
                sp.dma_start(hx_d[SEQ:SEQ + P, :], zero).then_inc(e_st, 16)
                sp.dma_start(acc_d[SEQ:SEQ + P, :], zero[:, 0:D]).then_inc(e_st, 16)
                sp.wait_ge(e_gd, 1)
                sp.dma_start(hx_d[0:SEQ, D:HX].rearrange("(t p) e -> p t e", p=P),
                             G.rearrange("p (t e) -> p t e", t=NT)).then_inc(e_st, 16)
                sp.wait_ge(e_st, 48)
                sp.wait_ge(e_slot, 16)

            @block.tensor
            def _(pe):
                pe.wait_ge(e_par, 80)
                for t in range(NT):
                    for k in range(KD):
                        last = nc.tensor.matmul(PS[:, 0, t * NE:(t + 1) * NE], hT[:, k, t * P:(t + 1) * P], wr[:, k, :],
                                                start=(k == 0), stop=(k == KD - 1))
                last.then_inc(e_lg, 1)
                pe.wait_ge(e_msk, 1)
                nc.tensor.matmul(PS[:, 1, :], strict, rep, start=True, stop=True)
                nc.tensor.matmul(PS[:, 2, :], ones, rep, start=True, stop=True).then_inc(e_tot, 1)
                pe.wait_ge(e_cols, 1)
                nc.tensor.matmul(PS[0:1, 3, 0:P], e_col[:, 0:1], ident, start=True, stop=True)
                nc.tensor.matmul(PS[0:1, 3, P:2 * P], e_col[:, 1:2], ident, start=True, stop=True)
                nc.tensor.matmul(PS[0:1, 3, 2 * P:2 * P + 1], e_col[:, 2:3], ones[:, 0:1], start=True, stop=True)\
                    .then_inc(e_rows, 1)

            @block.scalar
            def _(act):
                act.wait_ge(e_lg, 1)
                nc.scalar.activation(sc, PS[:, 0, :], ACT.Sigmoid).then_inc(e_sc, 1)

            @block.vector
            def _(v):
                link = chained(v, e_chain)
                nc.vector.memset(one_e, 1.0)
                link(nc.vector.memset(alt, 1.0))
                nc.vector.memset(alt.rearrange("p (i s) -> p i s", s=2)[:, :, 1], -1.0)
                nc.vector.memset(ones, 1.0)
                link(nc.vector.tensor_tensor(strict, upper, ident, ALU.subtract))
                nc.vector.memset(zero, 0.0).then_inc(e_zero, 1)
                v.wait_ge(e_sc, 1)
                v.wait_ge(e_par, 80)
                s3 = sel.rearrange("p (t e) -> p t e", t=NT)
                link(nc.vector.tensor_tensor(s3, sc.rearrange("p (t e) -> p t e", t=NT),
                                             rb.unsqueeze(1).broadcast_to([P, NT, NE]), ALU.add))
                for i in range(NT * NG):
                    last = nc.vector.max(m8[:, i * 8:(i + 1) * 8], sel[:, i * 8:(i + 1) * 8])
                link(last)
                m3 = m8.rearrange("p (i e) -> p i e", e=8)
                link(nc.vector.tensor_tensor(gsc, m3[:, :, 0], m3[:, :, 1], ALU.add))
                g3 = gsc.rearrange("p (t g) -> p t g", t=NT)
                mine = g3.unsqueeze(3).broadcast_to([P, NT, NG, NG])
                other = g3.unsqueeze(2).broadcast_to([P, NT, NG, NG])
                nc.vector.tensor_tensor(v4(cmp_), other, mine, ALU.is_gt)
                link(nc.vector.tensor_tensor(v4(eqv), other, mine, ALU.is_equal))
                link(nc.vector.tensor_tensor(eqv, eqv, ltg, ALU.mult))
                link(nc.vector.tensor_tensor(cmp_, cmp_, eqv, ALU.add))
                link(nc.vector.tensor_reduce(rank, cmp_.rearrange("p (i g) -> p i g", g=NG), AX.X, ALU.add))
                link(nc.vector.tensor_scalar(gmask, rank, 3.5, None, ALU.is_lt))
                gm = gmask.rearrange("p (t g) -> p t g", t=NT).unsqueeze(3).broadcast_to([P, NT, NG, GS])
                link(nc.vector.tensor_tensor(v4(sel), v4(sel), gm, ALU.mult))
                link(nc.vector.tensor_scalar(gmask, gmask, -1.0, 1e30, ALU.add, ALU.mult))
                link(nc.vector.tensor_tensor(v4(sel), v4(sel), gm, ALU.add))
                for t in range(NT):
                    link(nc.vector.max(t8[:, t * 8:(t + 1) * 8], sel[:, t * NE:(t + 1) * NE]))
                    link(nc.vector.match_replace(rep[:, t * NE:(t + 1) * NE], t8[:, t * 8:(t + 1) * 8],
                                                 sel[:, t * NE:(t + 1) * NE], -3e30))
                nc.vector.tensor_scalar(rep, rep, -2e30, None, ALU.is_lt).then_inc(e_msk, 1)
                v.wait_ge(e_msk, 1)
                link(nc.vector.tensor_tensor(G, sc, rep, ALU.mult))
                G3 = G.rearrange("p (t e) -> p t e", t=NT)
                link(nc.vector.tensor_reduce(den, G3, AX.X, ALU.add))
                link(nc.vector.reciprocal(den, den))
                link(nc.vector.tensor_scalar(den, den, ROUTED_SCALE, None, ALU.mult))
                nc.vector.tensor_tensor(G3, G3, den.unsqueeze(2).broadcast_to([P, NT, NE]), ALU.mult).then_inc(e_gd, 1)
                v.wait_ge(e_tot, 1)
                off3 = off.rearrange("p (t e) -> p t e", t=NT)
                link(nc.vector.tensor_copy(tot, PS[:, 2, :]))
                tot3 = tot.rearrange("p (t e) -> p t e", t=NT)
                link(nc.vector.memset(off3[:, 0, :], 0.0))
                for t in range(1, NT):
                    link(nc.vector.tensor_tensor(off3[:, t, :], off3[:, t - 1, :], tot3[:, t - 1, :], ALU.add))
                link(nc.vector.tensor_tensor(cnt, off3[:, NT - 1, :], tot3[:, NT - 1, :], ALU.add))
                link(nc.vector.tensor_copy(nblk, one_e))
                for j in range(1, NT):
                    link(nc.vector.scalar_tensor_tensor(nblk, cnt, float(j * P), nblk, ALU.is_gt, ALU.add))
                link(nc.vector.tensor_tensor_scan(cnt, one_e, nblk, 0.0, ALU.mult, ALU.add))
                link(nc.vector.tensor_tensor(bstart, cnt, nblk, ALU.subtract))
                blk_no = tok_id[:, 0:1]
                link(nc.vector.tensor_scalar(upto, bstart, blk_no, None, ALU.is_le))
                link(nc.vector.tensor_reduce(e_col[:, 0:1], upto, AX.X, ALU.add))
                link(nc.vector.tensor_scalar(e_col[:, 0:1], e_col[:, 0:1], -1.0, None, ALU.add))
                link(nc.vector.tensor_tensor(upto, upto, alt, ALU.mult))
                link(nc.vector.tensor_reduce(e_col[:, 1:2], upto, AX.X, ALU.add))
                link(nc.vector.tensor_scalar(e_col[:, 1:2], e_col[:, 1:2], -1.0, 1.0, ALU.mult, ALU.add))
                link(nc.vector.tensor_scalar(e_col[:, 3:4], blk_no, 2.0, None, ALU.mult))
                nc.vector.tensor_scalar(e_col[:, 2:3], e_col[:, 3:4], cnt[:, NE - 1:NE], None, ALU.is_lt).then_inc(e_cols, 1)
                link(nc.vector.tensor_copy(bounds[:, 0:NE], bstart))
                link(nc.vector.tensor_copy(bounds[:, NE:NE + 1], cnt[:, NE - 1:NE]))
                link(nc.vector.tensor_tensor(off, off, PS[:, 1, :], ALU.add))
                link(nc.vector.scalar_tensor_tensor(off3, bstart.unsqueeze(1).broadcast_to([P, NT, NE]), float(P), off3,
                                                    ALU.mult, ALU.add))
                link(nc.vector.scalar_tensor_tensor(off, off, 1.0, rep, ALU.add, ALU.mult))
                for t in range(NT):
                    last = nc.vector.max(t8[:, t * 8:(t + 1) * 8], off[:, t * NE:(t + 1) * NE])
                link(last)
                link(nc.vector.tensor_scalar(pos_i, t8, -1.0, None, ALU.add))
                v.wait_ge(e_rows, 1)
                nc.vector.tensor_copy(blk_e[0:1, 1:P + 1], PS[0:1, 3, 0:P])
                nc.vector.tensor_copy(blk_s[0:1, 1:P + 1], PS[0:1, 3, P:2 * P])
                nc.vector.memset(blk_e[0:1, 0:1], 0)
                nc.vector.memset(blk_s[0:1, 0:1], 0)
                link(nc.vector.tensor_copy(pairs[0:1, 0:1], PS[0:1, 3, 2 * P:2 * P + 1]))
                v.wait_ge(e_h, 16)
                for t in range(NT):
                    link(nc.vector.tensor_scalar(acc[:, t, :], acc[:, t, :], ALPHA, None, ALU.mult))

        top[0] = after_acc
        gu = carve(KD * 2 * FF).rearrange("p (k n) -> p k n", k=KD)
        dn = carve(2 * D).rearrange("p (f n) -> p f n", f=2)
        hid = carve(2 * SEQ).rearrange("p (f s) -> p f s", f=2)
        sl = [carve(HALF) for _ in range(2)]
        wg = carve(KD * D).rearrange("p (k n) -> p k n", k=KD)
        we = carve(2 * D).rearrange("p (f n) -> p f n", f=2)
        pt = carve(NT * PLE).rearrange("p (t n) -> p t n", t=NT)
        pT = carve(2 * SEQ).rearrange("p (f s) -> p f s", f=2)
        bg_row = carve(D)
        slot_f = carve(P)
        f_slot, f_sl2, f_stp, f_int = sem("f_slots"), sem("f_slots_in"), sem("f_slots_t"), sem("f_slots_int")
        pg = [carve(HALF) for _ in range(2)]
        f_w, f_wg, f_p, f_par = sem("f_w"), sem("f_wg"), sem("f_p"), sem("f_par")
        (f_gu, f_sl, f_hid, f_dn, f_acc, f_tp, f_pT, f_pl, f_lg, f_sg, f_pr, f_chain, f_stat, f_rstd, f_out, f_st) = (
            sem("f_" + n) for n in ("gu", "sl", "hid", "dn", "acc", "tp", "pT", "pl", "lg", "sg", "pr", "chain", "stat",
                                    "rstd", "out", "st"))
        with nc.Block() as block:
            @block.sync
            def _(sp):
                sp.dma_start(gu, a["sh_w_gu"].rearrange("(k p) n -> p k n", p=P)).then_inc(f_w, 16)
                sp.dma_start(dn, a["sh_w_down"].rearrange("(f p) n -> p f n", p=P)).then_inc(f_w, 16)
                sp.dma_start(pt, a["p"].rearrange("(t p) n -> p t n", p=P)).then_inc(f_p, 16)
                sp.dma_start(wg, a["ple_w_g"].rearrange("(k p) n -> p k n", p=P)).then_inc(f_wg, 16)
                sp.dma_start(we, a["ple_w_e"].rearrange("(f p) n -> p f n", p=P)).then_inc(f_wg, 16)
                sp.dma_start(bg_row, row("ple_b_g", 0, D)).then_inc(f_par, 16)
                sp.wait_ge(f_slot, 16 * NT * TOPK)
                sp.dma_start(slot_f, slot_d.rearrange("(b p) a -> b (p a)", p=P)).then_inc(f_sl2, 16)
                sp.wait_ge(f_pr, 2 * NT)
                sp.dma_start(acc_d[0:SEQ, :].rearrange("(t p) d -> p t d", p=P), acc).then_inc(f_st, 16)
                sp.wait_ge(f_st, 16)

            @block.tensor
            def _(pe):
                pe.wait_ge(f_w, 32)
                for q in range(4):
                    half, f = q // 2, q % 2
                    if q >= 2:
                        pe.wait_ge(f_hid, q - 1)
                    for part in range(2):
                        for k in range(KD):
                            last = nc.tensor.matmul(PS[:, 2 * (q % 2) + part, :],
                                                    gu[:, k, part * FF + f * P:part * FF + (f + 1) * P],
                                                    hT[:, k, half * HALF:(half + 1) * HALF], start=(k == 0), stop=(k == KD - 1))
                    last.then_inc(f_gu, 1)
                pe.wait_ge(f_p, 16)
                for t in range(0, NT, 2):
                    if t >= 4:
                        pe.wait_ge(f_pT, t // 2 - 1)
                    for c in range(4):
                        tt, f = t + c // 2, c % 2
                        last = nc.tensor.transpose(PS[:, 4 + (t // 2) % 2, c * P:(c + 1) * P], pt[:, tt, f * P:(f + 1) * P], ident)
                    last.then_inc(f_tp, 1)
                pe.wait_ge(f_hid, 4)
                for q in range(2 * NT):
                    t, j = q // 2, q % 2
                    if q >= 2:
                        pe.wait_ge(f_acc, q - 1)
                    for f in range(2):
                        last = nc.tensor.matmul(PS[:, 6 + q % 2, :], hid[:, f, t * P:(t + 1) * P],
                                                dn[:, f, j * HALF:(j + 1) * HALF], start=(f == 0), stop=(f == 1))
                    last.then_inc(f_dn, 1)
                pe.wait_ge(f_wg, 32)
                pe.wait_ge(f_pT, 4)
                for q in range(2 * NT):
                    t, j = q // 2, q % 2
                    js = slice(j * HALF, (j + 1) * HALF)
                    if q >= 2:
                        pe.wait_ge(f_pr, q - 1)
                    for k in range(KD):
                        last = nc.tensor.matmul(PS[:, q % 2, :], hT[:, k, t * P:(t + 1) * P], wg[:, k, js],
                                                start=(k == 0), stop=(k == KD - 1))
                    last.then_inc(f_pl, 1)
                    for f in range(2):
                        last = nc.tensor.matmul(PS[:, 2 + q % 2, :], pT[:, f, t * P:(t + 1) * P], we[:, f, js],
                                                start=(f == 0), stop=(f == 1))
                    last.then_inc(f_pl, 1)
                pe.wait_ge(f_sl2, 16)
                nc.tensor.transpose(PS[:, 4, 0:P], slot_f, ident).then_inc(f_stp, 1)

            @block.scalar
            def _(act):
                for q in range(4):
                    act.wait_ge(f_gu, q + 1)
                    if q >= 2:
                        act.wait_ge(f_hid, q - 1)
                    nc.scalar.activation(sl[q % 2], PS[:, 2 * (q % 2), :], ACT.Silu).then_inc(f_sl, 1)
                for i in range(NT // 2):
                    act.wait_ge(f_tp, i + 1)
                    nc.scalar.activation(pT[:, :, 2 * i * P:(2 * i + 2) * P].rearrange("p f (t s) -> p t f s", t=2),
                                         PS[:, 4 + i % 2, :].rearrange("p (t f s) -> p t f s", t=2, f=2),
                                         ACT.Copy).then_inc(f_pT, 1)
                for q in range(2 * NT):
                    act.wait_ge(f_lg, q + 1)
                    nc.scalar.activation(pg[q % 2], pg[q % 2], ACT.Sigmoid).then_inc(f_sg, 1)

            @block.vector
            def _(v):
                link = chained(v, f_chain)
                for q in range(4):
                    half, f = q // 2, q % 2
                    v.wait_ge(f_sl, q + 1)
                    nc.vector.tensor_tensor(hid[:, f, half * HALF:(half + 1) * HALF], sl[q % 2], PS[:, 2 * (q % 2) + 1, :],
                                            ALU.mult).then_inc(f_hid, 1)
                for q in range(2 * NT):
                    t, j = q // 2, q % 2
                    v.wait_ge(f_dn, q + 1)
                    dst = acc[:, t, j * HALF:(j + 1) * HALF]
                    nc.vector.tensor_tensor(dst, dst, PS[:, 6 + q % 2, :], ALU.add).then_inc(f_acc, 1)
                v.wait_ge(f_par, 16)
                v.wait_ge(f_acc, 2 * NT)

                def logits(q):
                    j = q % 2
                    v.wait_ge(f_pl, 2 * q + 1)
                    if q >= 2:
                        v.wait_ge(f_pr, q - 1)
                    nc.vector.tensor_tensor(pg[q % 2], PS[:, q % 2, :], bg_row[:, j * HALF:(j + 1) * HALF],
                                            ALU.add).then_inc(f_lg, 1)

                logits(0)
                for q in range(2 * NT):
                    t, j = q // 2, q % 2
                    v.wait_ge(f_pl, 2 * q + 2)
                    v.wait_ge(f_sg, q + 1)
                    link(nc.vector.tensor_tensor(pg[q % 2], pg[q % 2], PS[:, 2 + q % 2, :], ALU.mult))
                    dst = acc[:, t, j * HALF:(j + 1) * HALF]
                    nc.vector.tensor_tensor(dst, dst, pg[q % 2], ALU.add).then_inc(f_pr, 1)
                    if q + 1 < 2 * NT:
                        logits(q + 1)
                v.wait_ge(f_stp, 1)
                nc.vector.tensor_copy(slot_i[:, 1:MAXB + 1], PS[:, 4, 0:P])
                for i in (0, MAXB + 1, MAXB + 2):
                    last = nc.vector.tensor_scalar(slot_i[:, i:i + 1], tok_id[:, 0:1], float(SEQ), None, ALU.add)
                last.then_inc(f_int, 1)

            @block.gpsimd
            def _(pool):
                for t in range(NT):
                    for k in range(TOPK):
                        nc.gpsimd.indirect_dma_start(
                            out=slot_d, out_offset=bass.IndirectOffsetOnAxis(ap=pos_i[:, t * TOPK + k:t * TOPK + k + 1], axis=0),
                            in_=tok_id[:, t:t + 1], in_offset=None).then_inc(f_slot, 16)

        end_stage()
        top[0] = after_acc
        gu = carve(2 * KD * 2 * FF)
        dn = carve(2 * 2 * D)
        GU, DN = KD * 2 * FF, 2 * D
        xg = [carve(HX) for _ in range(2)]
        xT = [carve(KD * P) for _ in range(2)]
        gates = [carve(2)[:, 0:1] for _ in range(2)]
        hid = carve(2 * P)
        hidT = [carve(2 * P) for _ in range(2)]
        yo = [carve(D) for _ in range(2)]
        act_g = carve(2 * P)
        g_idx, s_idx = carve(2).bitcast(I32)[:, 0:1], carve(2).bitcast(I32)[:, 0:1]
        spare = carve(2)[:, 0:1]
        (x_wg, x_wd, x_idx, x_first, x_in, x_gate, x_xt, x_xa, x_xv, x_gu, x_sl, x_hid, x_ht, x_htc, x_dn, x_y,
         x_out) = (sem("x_" + n) for n in ("wg", "wd", "idx", "first", "in", "gate", "xt", "xa", "xv", "gu", "sl", "hid",
                                           "ht", "htc", "dn", "y", "out"))
        gu_v = a["exp_w_gu"].rearrange("e (k p) n -> e p k n", p=P)
        dn_v = a["exp_w_down"].rearrange("e (f p) n -> e p f n", p=P)

        def table(eng, ap, i, most):
            return eng.value_load(ap[0:1, bass.ds(i, 1)], min_val=0, max_val=most)

        def n_pairs(eng):
            return eng.value_load(pairs[0:1, 0:1], min_val=1, max_val=MAXB // 2)

        with nc.Block() as block:
            @block.sync
            def _(sp):
                def load(wait, e, u):
                    done = table(sp, bounds, e - 1, MAXB) if wait == 2 else None
                    if wait:
                        sp.wait_ge(x_wg, 16 * e)
                    if wait == 2:
                        sp.wait_ge(x_gu, done)
                    sp.dma_start(gu[:, u * GU:(u + 1) * GU].rearrange("p (k n) -> p k n", k=KD),
                                 gu_v[bass.ds(e, 1)].rearrange("a p k n -> p (a k) n")).then_inc(x_wg, 16)
                    if wait:
                        sp.wait_ge(x_wd, 16 * e)
                    if wait == 2:
                        sp.wait_ge(x_dn, 2 * done + 2)
                    sp.dma_start(dn[:, u * DN:(u + 1) * DN].rearrange("p (f n) -> p f n", f=2),
                                 dn_v[bass.ds(e, 1)].rearrange("a p f n -> p (a f) n")).then_inc(x_wd, 16)

                load(0, 0, 0)
                load(1, 1, 1)
                with sp.Fori(1, NE // 2) as i:
                    for u in range(2):
                        load(2, 2 * i + u, u)

            @block.gpsimd
            def _(pool):
                def gather(slot):
                    nc.gpsimd.indirect_dma_start(out=xg[slot], out_offset=None, in_=hx_d,
                                                 in_offset=bass.IndirectOffsetOnAxis(ap=g_idx, axis=0)).then_inc(x_in, 16)

                def add_rows(slot):
                    nc.gpsimd.indirect_dma_start(out=acc_d, out_offset=bass.IndirectOffsetOnAxis(ap=s_idx, axis=0),
                                                 in_=yo[slot], in_offset=None, compute_op=ALU.add).then_inc(x_out, 16)

                for i in range(2):
                    nc.gpsimd.dma_start(spare, a["pad_id"].rearrange("(p a) -> p a", p=P)).then_inc(x_out, 16)
                    pool.wait_ge(x_out, 16 * i + 16)
                for i in range(2):
                    nc.gpsimd.tensor_copy(g_idx, slot_i[:, i + 1:i + 2]).then_inc(x_first, 1)
                    pool.wait_ge(x_first, i + 1)
                    gather(i)
                    pool.wait_ge(x_in, 16 * i + 16)
                n = n_pairs(pool)
                with pool.Fori(0, n) as i:
                    for s in range(2):
                        b = 2 * i + s
                        pool.wait_ge(x_in, 16 * b + 32)
                        pool.nop(nofuse=True)
                        nc.gpsimd.tensor_copy(g_idx, slot_i[:, bass.ds(b + 3, 1)]).then_inc(x_idx, 1)
                        pool.wait_ge(x_xt, b + 1)
                        pool.wait_ge(x_gate, b + 2)
                        pool.wait_ge(x_idx, 2 * b + 1)
                        pool.nop(nofuse=True)
                        gather(s)
                        pool.wait_ge(x_out, 16 * b + 32)
                        pool.nop(nofuse=True)
                        nc.gpsimd.tensor_copy(s_idx, slot_i[:, bass.ds(b, 1)]).then_inc(x_idx, 1)
                        pool.wait_ge(x_y, 2 * b + 4)
                        pool.wait_ge(x_idx, 2 * b + 2)
                        pool.nop(nofuse=True)
                        add_rows(1 - s)
                pool.wait_ge(x_out, 32 * n + 32)
                pool.nop(nofuse=True)
                nc.gpsimd.tensor_copy(s_idx, slot_i[:, bass.ds(2 * n, 1)]).then_inc(x_idx, 1)
                pool.wait_ge(x_y, 4 * n + 4)
                pool.wait_ge(x_idx, 4 * n + 1)
                pool.nop(nofuse=True)
                add_rows(1)
                pool.wait_ge(x_in, 32 * n + 32)
                pool.wait_ge(x_out, 32 * n + 48)
                pool.nop(nofuse=True)

            @block.tensor
            def _(pe):
                def transpose_block(slot):
                    for k in range(KD):
                        last = nc.tensor.transpose(PS[:, k // 4, (k % 4) * P:(k % 4 + 1) * P], xg[slot][:, k * P:(k + 1) * P],
                                                   ident)
                    last.then_inc(x_xt, 1)

                def down(hslot, weights):
                    for j in range(2):
                        for f in range(2):
                            last = nc.tensor.matmul(PS[:, 5 + j, :], hidT[hslot][:, f * P:(f + 1) * P],
                                                    dn[:, bass.ds(weights * DN + (f * D + j * HALF), HALF)],
                                                    start=(f == 0), stop=(f == 1))
                        last.then_inc(x_dn, 1)

                n = n_pairs(pe)
                pe.wait_ge(x_in, 16)
                transpose_block(0)
                with pe.Fori(0, n) as i:
                    for s in range(2):
                        b = 2 * i + s
                        expert, weights = table(pe, blk_e, b + 1, NE - 1), table(pe, blk_s, b + 1, 1)
                        expert0, weights0 = table(pe, blk_e, b, NE - 1), table(pe, blk_s, b, 1)
                        pe.wait_ge(x_wg, 16 * expert + 16)
                        pe.wait_ge(x_xa, b + 1)
                        pe.wait_ge(x_xv, b + 1)
                        pe.wait_ge(x_hid, b + 1)
                        for k in range(KD):
                            last = nc.tensor.matmul(PS[:, 2 + s, :], xT[s][:, k * P:(k + 1) * P],
                                                    gu[:, bass.ds(weights * GU + k * 2 * FF, 2 * FF)],
                                                    start=(k == 0), stop=(k == KD - 1))
                        last.then_inc(x_gu, 1)
                        pe.wait_ge(x_in, 16 * b + 32)
                        transpose_block(1 - s)
                        pe.wait_ge(x_htc, b + 1)
                        pe.wait_ge(x_wd, 16 * expert0 + 16)
                        pe.wait_ge(x_y, 2 * b + 2)
                        down(1 - s, weights0)
                        pe.wait_ge(x_hid, b + 2)
                        for f in range(2):
                            last = nc.tensor.transpose(PS[:, 4, f * P:(f + 1) * P], hid[:, f * P:(f + 1) * P], ident)
                        last.then_inc(x_ht, 1)
                weights0 = table(pe, blk_s, 2 * n, 1)
                pe.wait_ge(x_wd, 16 * NE)
                pe.wait_ge(x_htc, 2 * n + 1)
                pe.wait_ge(x_y, 4 * n + 2)
                down(1, weights0)

            @block.scalar
            def _(act):
                act.wait_ge(x_xt, 1)
                nc.scalar.activation(xT[0][:, 0:HALF], PS[:, 0, :], ACT.Copy).then_inc(x_xa, 1)

                def out_half(b, slot):
                    act.wait_ge(x_out, 16 * b + 16)
                    act.wait_ge(x_gate, b + 1)
                    act.wait_ge(x_dn, 2 * b + 1)
                    nc.scalar.activation(yo[slot][:, 0:HALF], PS[:, 5, :], ACT.Copy, scale=gates[slot]).then_inc(x_y, 1)

                n = n_pairs(act)
                with act.Fori(0, n) as i:
                    for s in range(2):
                        b = 2 * i + s
                        act.wait_ge(x_hid, b + 1)
                        act.wait_ge(x_gu, b + 1)
                        nc.scalar.activation(act_g, PS[:, 2 + s, 0:FF], ACT.Silu).then_inc(x_sl, 1)
                        act.wait_ge(x_xt, b + 2)
                        nc.scalar.activation(xT[1 - s][:, 0:HALF], PS[:, 0, :], ACT.Copy).then_inc(x_xa, 1)
                        out_half(b, 1 - s)
                        act.wait_ge(x_ht, b + 1)
                        nc.scalar.activation(hidT[s], PS[:, 4, 0:2 * P], ACT.Copy).then_inc(x_htc, 1)
                out_half(2 * n, 1)

            @block.vector
            def _(v):
                v.sem_inc(x_hid, 1)
                v.sem_inc(x_y, 2)
                nc.vector.memset(hidT[1], 0.0).then_inc(x_htc, 1)
                nc.vector.memset(gates[1], 0.0).then_inc(x_gate, 1)
                v.wait_ge(x_xt, 1)
                nc.vector.tensor_copy(xT[0][:, HALF:2 * HALF], PS[:, 1, :]).then_inc(x_xv, 1)

                def out_half(b, slot):
                    v.wait_ge(x_out, 16 * b + 16)
                    v.wait_ge(x_gate, b + 1)
                    v.wait_ge(x_dn, 2 * b + 2)
                    nc.vector.tensor_scalar(yo[slot][:, HALF:2 * HALF], PS[:, 6, :], gates[slot], None, ALU.mult)\
                        .then_inc(x_y, 1)

                n = n_pairs(v)
                with v.Fori(0, n) as i:
                    for s in range(2):
                        b = 2 * i + s
                        expert = table(v, blk_e, b + 1, NE - 1)
                        v.wait_ge(x_in, 16 * b + 16)
                        v.wait_ge(x_y, 2 * b + 2)
                        nc.vector.tensor_scalar(gates[s], xg[s][:, bass.ds(expert + D, 1)], 1.0, None, ALU.mult)\
                            .then_inc(x_gate, 1)
                        v.wait_ge(x_sl, b + 1)
                        nc.vector.tensor_tensor(hid, act_g, PS[:, 2 + s, FF:2 * FF], ALU.mult).then_inc(x_hid, 1)
                        v.wait_ge(x_xt, b + 2)
                        nc.vector.tensor_copy(xT[1 - s][:, HALF:2 * HALF], PS[:, 1, :]).then_inc(x_xv, 1)
                        out_half(b, 1 - s)
                out_half(2 * n, 1)

        top[0] = after_acc
        g_row, b_row = carve(D), carve(D)
        st = carve(NT * 12).rearrange("p (t j s) -> p t j s", t=NT, j=2)
        mv = carve(NT * 2).rearrange("p (t s) -> p t s", t=NT)
        rstd = carve(NT)
        n_par, n_in = sem("n_par"), [sem(f"n_in{i}") for i in range(4)]
        n_chain, n_stat, n_rstd, n_out, n_st = (sem("n_" + n) for n in ("chain", "stat", "rstd", "out", "st"))
        with nc.Block() as block:
            @block.sync
            def _(sp):
                av = acc_d[0:SEQ, :].rearrange("(t p) d -> p t d", p=P)
                for i in range(4):
                    sp.dma_start(acc[:, 2 * i:2 * i + 2, :], av[:, 2 * i:2 * i + 2, :]).then_inc(n_in[i], 16)
                sp.dma_start(g_row, row("ln2_g", 0, D)).then_inc(n_par, 16)
                sp.dma_start(b_row, row("ln2_b", 0, D)).then_inc(n_par, 16)
                ov = out[0].rearrange("(t p) d -> t p d", p=P)
                for t in range(NT):
                    sp.wait_ge(n_out, t + 1)
                    sp.dma_start(ov[t], acc[:, t, :]).then_inc(n_st, 16)
                sp.wait_ge(n_st, 16 * NT)

            @block.vector
            def _(v):
                link = chained(v, n_chain)
                for t in range(NT):
                    v.wait_ge(n_in[t // 2], 16)
                    ln_stats(v, link, acc, st, mv, t).then_inc(n_stat, 1)
                v.wait_ge(n_par, 32)
                for t in range(NT):
                    v.wait_ge(n_rstd, 2 * (t + 1))
                    ln_apply(link, acc, t, mv, rstd, g_row, b_row).then_inc(n_out, 1)

            @block.gpsimd
            def _(pool):
                for t in range(NT):
                    pool.wait_ge(n_stat, t + 1)
                    nc.gpsimd.tensor_scalar(rstd[:, t:t + 1], mv[:, t, 1:2], LN_EPS, None, ALU.add).then_inc(n_rstd, 1)
                    pool.wait_ge(n_rstd, 2 * t + 1)
                    nc.gpsimd.tensor_tensor(rstd[:, t:t + 1], rstd[:, t:t + 1], nhalf[:, 0:1], ALU.pow).then_inc(n_rstd, 1)


def lay_out(inputs):
    f = {n: np.ascontiguousarray(np.asarray(x)) for n, x in inputs.items()}
    one = {n: (x if n in ("x", "p", "ln_in_g", "ln_in_b") else x[0]) for n, x in f.items()}
    one["p"] = f["p"][0, 0]
    cols = np.zeros((P, N_COLS), np.float32)

    def put(name, v):
        at, n = COLS[name]
        cols[:, at:at + n] = np.reshape(v, (n, P)).T

    b = one["b_in"]
    put("b_rg", b[C_RG:C_RG + W])
    put("b_qkv", b[C_QKV:C_QKV + 3 * W])
    put("b_gg", b[C_GG:C_GG + W])
    put("b_lx", b[C_LX:C_LX + W])
    put("b_lg", b[C_LG:C_LG + W])
    put("b_mg", b[C_MG:C_MG + 3 * D])
    put("ret_g", one["ret_norm_g"])
    put("ret_b", one["ret_norm_b"])
    put("gdn_w", one["gdn_conv_w"])
    put("gdn_g", one["gdn_norm_g"])
    put("lru_w", one["lru_conv_w"])
    put("lru_cb", one["lru_conv_b"])
    put("lru_br", one["lru_b_r"])
    put("lru_bi", one["lru_b_i"])
    put("lru_lam", one["lru_lambda"])
    one["cols"] = cols
    one["consts"] = constant_table()
    before = np.broadcast_to(np.arange(NG)[None, :] < np.arange(NG)[:, None], (NT, NG, NG))
    one["before"] = before.reshape(-1).astype(np.float32)
    one["token_id"] = np.arange(SEQ, dtype=np.float32).reshape(NT, P).T
    one["pad_id"] = np.arange(SEQ, SEQ + P, dtype=np.float32)
    for n in ("ret_norm_g", "ret_norm_b", "gdn_conv_w", "gdn_norm_g", "lru_conv_w", "lru_conv_b", "lru_b_r",
              "lru_b_i", "lru_lambda"):
        del one[n]
    return {n: np.ascontiguousarray(x) for n, x in one.items()}


def kernel(**inputs):
    import concourse.bacc as _bacc
    from concourse.bass_utils import run_bass_kernel_spmd as _run

    nc = _bacc.Bacc("TRN2", target_bir_lowering=False, num_devices=1)
    arrays = lay_out(inputs)
    a = {n: nc.dram_tensor(f"in_{n}", x.shape, F32, kind="ExternalInput").ap() for n, x in arrays.items()}
    out = nc.dram_tensor("out", (1, SEQ, D), F32, kind="ExternalOutput").ap()
    build(nc, a, out)
    r = _run(nc, [{f"in_{n}": x for n, x in arrays.items()}], core_ids=[0])
    return r.results[0]["out"]
```
